# Optimizing a Trainium2 kernel written in Bass

```python
import math
import jax, jax.numpy as jnp
from jax import lax
import numpy as np

D_MODEL = 1024
BATCH = 1
SEQ = 256
DEPTH = 2

GRID_W = 64
CTX_LEN = 256
EPS = 1e-6
H_A = 4
DK_A = 128
DV_A = 128
CONV_K = 5
CHUNK = 64
HQ_B = 8
HKV_B = 2
GQ_B = HQ_B // HKV_B
DH_B = 64
WINDOW = 128
BLK = 128
ROPE_THETA = 10000.0
N_EXPERTS = 16
N_GROUPS = 4
EXP_PER_GROUP = N_EXPERTS // N_GROUPS
GROUP_SCORE_TOPK = 2
TOP_K = 2
D_EXPERT = 512
QKV_A = 2 * H_A * DK_A + H_A * DV_A
IN_SPLITS = (QKV_A, H_A * DV_A, 2 * H_A, 2 * H_A, HQ_B * DH_B, HKV_B * DH_B, HKV_B * DH_B, D_MODEL, D_MODEL)
IN_WIDTH = sum(IN_SPLITS)

kernel_name = "hybrid_gdn_swa_moe_prefix_dit"

f32 = jnp.float32

def rmsnorm(x, g):
    xf = x.astype(f32)
    y = xf * lax.rsqrt(jnp.mean(xf * xf, axis=-1, keepdims=True) + EPS)
    return (y * g.astype(f32)).astype(x.dtype)

def l2norm(x):
    xf = x.astype(f32)
    return xf * lax.rsqrt(jnp.sum(xf * xf, axis=-1, keepdims=True) + EPS)

def adaln_params(cond, w_mod, b_mod):
    m = jax.nn.silu(cond) @ w_mod + b_mod
    return jnp.split(m[..., None, :], 6, axis=-1)

def modulate(h, shift, scale):
    return h * (1 + scale) + shift

def split_in(p):
    return jnp.split(p, [int(i) for i in np.cumsum(IN_SPLITS)[:-1]], axis=-1)

def short_conv_silu(u, w):
    C = u.shape[-1]
    y = lax.conv_general_dilated(u, w[:, None, :].astype(u.dtype), window_strides=(1,),
                                 padding=((CONV_K // 2, CONV_K // 2),),
                                 dimension_numbers=('NWC', 'WIO', 'NWC'), feature_group_count=C)
    return jax.nn.silu(y)

def gdn_chunked(q, k, v, g, beta, s0):
    q, k, v, g, beta = (t.astype(f32) for t in (q, k, v, g, beta))
    B_, L, H, _ = q.shape
    DV = v.shape[-1]
    n = L // CHUNK

    def chunks(t):
        return jnp.swapaxes(t.reshape((B_, n, CHUNK, H) + t.shape[3:]), 2, 3)

    qc, kc, vc, bc = chunks(q), chunks(k), chunks(v), chunks(beta)
    gc = jnp.cumsum(chunks(g), axis=-1)
    idx = jnp.arange(CHUNK)
    tril = idx[:, None] >= idx[None, :]
    strict = idx[:, None] > idx[None, :]
    decay = jnp.where(tril, jnp.exp(jnp.where(tril, gc[..., :, None] - gc[..., None, :], 0.0)), 0.0)
    kb = kc * bc[..., None]
    a_mat = jnp.where(strict, jnp.einsum('bnhid,bnhjd->bnhij', kb, kc) * decay, 0.0)
    lhs = a_mat + jnp.eye(CHUNK, dtype=f32)
    rhs = jnp.concatenate([vc * bc[..., None], kb * jnp.exp(gc)[..., None]], axis=-1)
    sol = lax.linalg.triangular_solve(lhs, rhs, left_side=True, lower=True, unit_diagonal=True)
    u, w = sol[..., :DV], sol[..., DV:]
    attn = jnp.where(tril, jnp.einsum('bnhid,bnhjd->bnhij', qc, kc) * decay, 0.0)
    qg = qc * jnp.exp(gc)[..., None]
    kg = kc * jnp.exp(gc[..., -1:] - gc)[..., None]
    glast = jnp.exp(gc[..., -1])
    xs = tuple(jnp.moveaxis(t, 1, 0) for t in (qg, kg, u, w, attn, glast))

    def step(S, inp):
        qg_, kg_, u_, w_, attn_, gl_ = inp
        v_new = u_ - jnp.einsum('bhck,bhkv->bhcv', w_, S)
        o = jnp.einsum('bhck,bhkv->bhcv', qg_, S) + jnp.einsum('bhij,bhjv->bhiv', attn_, v_new)
        S = S * gl_[..., None, None] + jnp.einsum('bhck,bhcv->bhkv', kg_, v_new)
        return S, o

    s_fin, o = lax.scan(step, s0.astype(f32), xs)
    o = jnp.swapaxes(jnp.moveaxis(o, 0, 1), 2, 3).reshape(B_, L, H, DV)
    return o, s_fin

def mixer_a(qkv, beta_raw, alpha_raw, z, conv_w, a_log, dt_bias, norm_g, s0_f, s0_b):
    B_, L, _ = qkv.shape
    qkv = short_conv_silu(qkv, conv_w)
    q, k, v = jnp.split(qkv, [H_A * DK_A, 2 * H_A * DK_A], axis=-1)
    q = l2norm(q.reshape(B_, L, H_A, DK_A)) * (DK_A ** -0.5)
    k = l2norm(k.reshape(B_, L, H_A, DK_A))
    v = v.reshape(B_, L, H_A, DV_A)
    beta = jax.nn.sigmoid(beta_raw.astype(f32)).reshape(B_, L, 2, H_A)
    g = -jnp.exp(a_log.astype(f32)) * jax.nn.softplus(alpha_raw.astype(f32).reshape(B_, L, 2, H_A) + dt_bias.astype(f32))
    o_f, s_f = gdn_chunked(q, k, v, g[:, :, 0], beta[:, :, 0], s0_f)
    flip = lambda t: jnp.flip(t, axis=1)
    o_b, s_b = gdn_chunked(flip(q), flip(k), flip(v), flip(g[:, :, 1]), flip(beta[:, :, 1]), s0_b)
    o = o_f + flip(o_b)
    o = rmsnorm(o, norm_g) * jax.nn.silu(z.astype(f32).reshape(B_, L, H_A, DV_A))
    return o.reshape(B_, L, H_A * DV_A).astype(qkv.dtype), s_f, s_b

def rope_1d(x, pos):
    nf = x.shape[-1] // 2
    inv = ROPE_THETA ** (-jnp.arange(nf, dtype=f32) / nf)
    ang = pos[:, None] * inv[None, :]
    cos = jnp.cos(ang)[None, :, None, :].astype(x.dtype)
    sin = jnp.sin(ang)[None, :, None, :].astype(x.dtype)
    x1, x2 = x[..., :nf], x[..., nf:]
    return jnp.concatenate([x1 * cos - x2 * sin, x1 * sin + x2 * cos], axis=-1)

def axial_rope(x, rows, cols):
    half = x.shape[-1] // 2
    return jnp.concatenate([rope_1d(x[..., :half], rows), rope_1d(x[..., half:], cols)], axis=-1)

def window_attn(q, k, v, kc, vc, sink):
    B_, L = q.shape[:2]
    Lc = kc.shape[1]
    nb = L // BLK
    nl = 3 * BLK
    qb = q.reshape(B_, nb, BLK, HKV_B, GQ_B, DH_B)

    def band(t):
        tp = jnp.pad(t, ((0, 0), (BLK, BLK), (0, 0), (0, 0))).reshape(B_, nb + 2, BLK, HKV_B, DH_B)
        return jnp.concatenate([tp[:, :-2], tp[:, 1:-1], tp[:, 2:]], axis=2)

    kw, vw = band(k), band(v)
    q_pos = jnp.arange(L).reshape(nb, BLK)
    k_pos = jnp.arange(nb)[:, None] * BLK - BLK + jnp.arange(nl)[None, :]
    kp = k_pos[:, None, :]
    valid = (jnp.abs(q_pos[:, :, None] - kp) <= WINDOW) & (kp >= 0) & (kp < L)
    scale = DH_B ** -0.5
    s_loc = jnp.einsum('bnqkgd,bnpkd->bnkgqp', qb, kw).astype(f32) * scale
    s_loc = jnp.where(valid[None, :, None, None], s_loc, -jnp.inf)
    s_ctx = jnp.einsum('bnqkgd,bckd->bnkgqc', qb, kc).astype(f32) * scale
    s_sink = jnp.broadcast_to(sink.astype(f32).reshape(1, 1, HKV_B, GQ_B, 1, 1), s_loc.shape[:-1] + (1,))
    p = jax.nn.softmax(jnp.concatenate([s_loc, s_ctx, s_sink], axis=-1), axis=-1).astype(v.dtype)
    o = (jnp.einsum('bnkgqp,bnpkd->bnqkgd', p[..., :nl], vw)
         + jnp.einsum('bnkgqc,bckd->bnqkgd', p[..., nl:nl + Lc], vc))
    return o.reshape(B_, L, HQ_B * DH_B)

def context_attn(q, k, v, sink):
    B_, Lc = q.shape[:2]
    qg = q.reshape(B_, Lc, HKV_B, GQ_B, DH_B)
    s = jnp.einsum('bqkgd,bpkd->bkgqp', qg, k).astype(f32) * (DH_B ** -0.5)
    s_sink = jnp.broadcast_to(sink.astype(f32).reshape(1, HKV_B, GQ_B, 1, 1), s.shape[:-1] + (1,))
    p = jax.nn.softmax(jnp.concatenate([s, s_sink], axis=-1), axis=-1)[..., :Lc].astype(v.dtype)
    o = jnp.einsum('bkgqp,bpkd->bqkgd', p, v)
    return o.reshape(B_, Lc, HQ_B * DH_B)

def merge_branches(ya, yb, gate_a, gate_b, w_oa, w_ob, w_o):
    return (jax.nn.sigmoid(gate_a) * (ya @ w_oa) + jax.nn.sigmoid(gate_b) * (yb @ w_ob)) @ w_o

def mix_tokens(h, hc, rows, cols, w_in, conv_w, a_log, dt_bias, gdn_g, sink, w_oa, w_ob, w_o, need_ctx):
    B_ = h.shape[0]
    qkv_a, z_a, b_a, a_a, q_b, k_b, v_b, gate_a, gate_b = split_in(h @ w_in)
    qkv_ac, z_ac, b_ac, a_ac, q_bc, k_bc, v_bc, gate_ac, gate_bc = split_in(hc @ w_in)
    s0 = jnp.zeros((B_, H_A, DK_A, DV_A), f32)
    ya_c, s_f, s_b = mixer_a(qkv_ac, b_ac, a_ac, z_ac, conv_w, a_log, dt_bias, gdn_g, s0, s0)
    ya, _, _ = mixer_a(qkv_a, b_a, a_a, z_a, conv_w, a_log, dt_bias, gdn_g, s_f, s_b)
    heads = lambda t, nh: t.reshape(t.shape[0], t.shape[1], nh, DH_B)
    q = axial_rope(heads(q_b, HQ_B), rows, cols)
    k = axial_rope(heads(k_b, HKV_B), rows, cols)
    kc, vc = heads(k_bc, HKV_B), heads(v_bc, HKV_B)
    yb = window_attn(q, k, heads(v_b, HKV_B), kc, vc, sink)
    y = merge_branches(ya, yb, gate_a, gate_b, w_oa, w_ob, w_o)
    if not need_ctx:
        return y, None
    yb_c = context_attn(heads(q_bc, HQ_B), kc, vc, sink)
    return y, merge_branches(ya_c, yb_c, gate_ac, gate_bc, w_oa, w_ob, w_o)

def moe(h, w_router, router_bias, w_gate, w_up, w_down):
    B_, L, D = h.shape
    t = h.reshape(B_ * L, D)
    scores = jax.nn.sigmoid((t @ w_router).astype(f32))
    sel = scores + router_bias.astype(f32)
    group_score = lax.top_k(sel.reshape(-1, N_GROUPS, EXP_PER_GROUP), GROUP_SCORE_TOPK)[0].sum(-1)
    g_idx = jnp.argmax(group_score, axis=-1)
    in_group = (jnp.arange(N_EXPERTS) // EXP_PER_GROUP)[None, :] == g_idx[:, None]
    _, e_idx = lax.top_k(jnp.where(in_group, sel, -jnp.inf), TOP_K)
    wts = jnp.take_along_axis(scores, e_idx, axis=-1)
    wts = wts / jnp.sum(wts, axis=-1, keepdims=True)
    combine = jnp.sum(jax.nn.one_hot(e_idx, N_EXPERTS, dtype=f32) * wts[..., None], axis=1).astype(h.dtype)
    out = jnp.zeros_like(t)
    for e in range(N_EXPERTS):
        he = jax.nn.silu(t @ w_gate[e]) * (t @ w_up[e])
        out = out + combine[:, e:e + 1] * (he @ w_down[e])
    return out.reshape(B_, L, D)

def setup_inputs(seed: int = 0) -> dict:
    key = jax.random.key(seed)
    ks = jax.random.split(key, 24)

    def nrm(k, shape, scale):
        return jax.random.normal(k, shape, f32) * scale

    dt = jnp.exp(jax.random.uniform(ks[11], (DEPTH, 2, H_A), f32, math.log(1e-3), math.log(1e-1)))
    return {
        "x": nrm(ks[0], (BATCH, SEQ, D_MODEL), 1.0),
        "c": nrm(ks[1], (BATCH, D_MODEL), 1.0),
        "ctx": nrm(ks[2], (BATCH, CTX_LEN, D_MODEL), 1.0),
        "c_ctx": nrm(ks[3], (D_MODEL,), 1.0),
        "w_mod": nrm(ks[4], (DEPTH, D_MODEL, 6 * D_MODEL), 0.5 * D_MODEL ** -0.5),
        "b_mod": nrm(ks[5], (DEPTH, 6 * D_MODEL), 0.02),
        "norm1_g": 1.0 + nrm(ks[6], (DEPTH, D_MODEL), 0.02),
        "norm2_g": 1.0 + nrm(ks[7], (DEPTH, D_MODEL), 0.02),
        "w_in": nrm(ks[8], (DEPTH, D_MODEL, IN_WIDTH), D_MODEL ** -0.5),
        "conv_w": nrm(ks[9], (DEPTH, CONV_K, QKV_A), CONV_K ** -0.5),
        "a_log": jnp.log(jax.random.uniform(ks[10], (DEPTH, 2, H_A), f32, 1.0, 16.0)),
        "dt_bias": dt + jnp.log(-jnp.expm1(-dt)),
        "gdn_norm_g": 1.0 + nrm(ks[12], (DEPTH, DV_A), 0.02),
        "sink": nrm(ks[13], (DEPTH, HQ_B), 0.5),
        "w_oa": nrm(ks[14], (DEPTH, H_A * DV_A, D_MODEL), (H_A * DV_A) ** -0.5),
        "w_ob": nrm(ks[15], (DEPTH, HQ_B * DH_B, D_MODEL), (HQ_B * DH_B) ** -0.5),
        "w_o": nrm(ks[16], (DEPTH, D_MODEL, D_MODEL), D_MODEL ** -0.5),
        "w_router": nrm(ks[17], (D_MODEL, N_EXPERTS), D_MODEL ** -0.5),
        "router_bias": nrm(ks[18], (N_EXPERTS,), 0.01),
        "w_gate": nrm(ks[19], (DEPTH, N_EXPERTS, D_MODEL, D_EXPERT), D_MODEL ** -0.5),
        "w_up": nrm(ks[20], (DEPTH, N_EXPERTS, D_MODEL, D_EXPERT), D_MODEL ** -0.5),
        "w_down": nrm(ks[21], (DEPTH, N_EXPERTS, D_EXPERT, D_MODEL), D_EXPERT ** -0.5),
        "final_g": 1.0 + nrm(ks[22], (D_MODEL,), 0.02),
    }

def reference(x, c, ctx, c_ctx, w_mod, b_mod, norm1_g, norm2_g, w_in, conv_w, a_log, dt_bias,
              gdn_norm_g, sink, w_oa, w_ob, w_o, w_router, router_bias, w_gate, w_up, w_down, final_g):
    L = x.shape[1]
    n_rows = L // GRID_W
    rows = jnp.repeat(jnp.arange(n_rows, dtype=f32), GRID_W)
    cols = jnp.tile(jnp.arange(GRID_W, dtype=f32), n_rows)
    xc = ctx
    for l in range(DEPTH):
        need_ctx = l < DEPTH - 1
        sh1, sc1, g1, sh2, sc2, g2 = adaln_params(c, w_mod[l], b_mod[l])
        csh1, csc1, cg1, csh2, csc2, cg2 = adaln_params(c_ctx, w_mod[l], b_mod[l])
        h = modulate(rmsnorm(x, norm1_g[l]), sh1, sc1)
        hc = modulate(rmsnorm(xc, norm1_g[l]), csh1, csc1)
        y, yc = mix_tokens(h, hc, rows, cols, w_in[l], conv_w[l], a_log[l], dt_bias[l], gdn_norm_g[l],
                           sink[l], w_oa[l], w_ob[l], w_o[l], need_ctx)
        x = x + g1 * y
        h = modulate(rmsnorm(x, norm2_g[l]), sh2, sc2)
        x = x + g2 * moe(h, w_router, router_bias, w_gate[l], w_up[l], w_down[l])
        if need_ctx:
            xc = xc + cg1 * yc
            hc = modulate(rmsnorm(xc, norm2_g[l]), csh2, csc2)
            xc = xc + cg2 * moe(hc, w_router, router_bias, w_gate[l], w_up[l], w_down[l])
    return rmsnorm(x, final_g)


_drawn_inputs = setup_inputs


def setup_inputs(seed=0):
    import zlib

    import numpy as np

    out = dict(_drawn_inputs(seed))
    spreads = {}
    factors = {'norm1_g': 4.958,
     'gdn_norm_g': 8.0,
     'sink': 8.0,
     'final_g': 7.994,
     'norm2_g': 6.289,
     'router_bias': 3.871}
    for name, (base, spread) in spreads.items():
        noise = np.random.default_rng([zlib.crc32(name.encode()), seed]).standard_normal(out[name].shape)
        drawn = base * np.exp(spread * noise) if base else spread * noise
        out[name] = __import__('jax').numpy.asarray(drawn.astype(out[name].dtype))
    for name, factor in factors.items():
        out[name] = (out[name] * factor).astype(out[name].dtype)
    return out
```

```python
from contextlib import ExitStack

import concourse.bass as bass
import numpy as np
from concourse import mybir

F32 = mybir.dt.float32
I32 = mybir.dt.int32
U32 = mybir.dt.uint32
ALU = mybir.AluOpType
ACT = mybir.ActivationFunctionType
AX = mybir.AxisListType

P = 128
D = 1024
KD = D // P
SEQ = 256
NT = 4
DEPTH = 2
EPS = 1e-6
HA = 4
HB, GB, DH = 8, 2, 64
NE, NG = 16, 4
FE = 512
KF = FE // P
CONV = 5
CHT = 12
GRID_W = 64
C_Z, C_BA, C_GA, C_GB, C_END = 1536, 2048, 2832, 3856, 4880
AROW = C_GA - C_BA
A_Q, A_K, A_V = 16, 528, 656
SLOTS = 4
LV = 7
NBLK = 24
SCALE = DH ** -0.5


def constants():
    i = np.arange(P)[:, None]
    j = np.arange(P)[None, :]
    parts = {"ident": i == j, "ones": np.ones((P, P)), "upper": i <= j, "lower": i >= j,
             "supper": i < j, "slower": i > j}
    for k in range(LV):
        parts[f"level{k}"] = (i >> (k + 1) == j >> (k + 1)) & ((i >> k) & 1 == 1) & ((j >> k) & 1 == 0)
    parts["level0T"] = parts["level0"].T
    nf = DH // 4
    inv = (np.float32(10000.0) ** (-np.arange(nf, dtype=np.float32) / np.float32(nf))).astype(np.float32)
    pos = np.arange(SEQ)
    ang = [(q.astype(np.float32)[:, None] * inv[None, :]).astype(np.float32) for q in (pos // GRID_W, pos % GRID_W)]
    cos = np.concatenate([np.cos(ang[0]), np.cos(ang[0]), np.cos(ang[1]), np.cos(ang[1])], 1)
    sin = np.concatenate([-np.sin(ang[0]), np.sin(ang[0]), -np.sin(ang[1]), np.sin(ang[1])], 1)
    for n in range(2):
        parts[f"cos{n}"] = cos[n * P:(n + 1) * P]
        parts[f"sin{n}"] = sin[n * P:(n + 1) * P]
    parts["band0"] = np.where(j <= i, 0.0, -1e30)
    parts["band1"] = np.where(i <= j, 0.0, -1e30)
    parts["iota"] = np.broadcast_to(j, (P, P))
    parts["token"] = i + P * np.arange(NT)[None, :]
    parts["grouprank"] = np.broadcast_to(8 - np.arange(NG), (P, NG))
    parts["expertrank"] = np.broadcast_to(32 - np.arange(NE), (P, NE))
    parts["eps"] = np.full((P, 1), EPS)
    at, off = {}, 0
    for k, v in parts.items():
        at[k] = (off, v.shape[1])
        off += v.shape[1]
    return np.concatenate([np.asarray(v, np.float32) for v in parts.values()], 1), at


def build(nc, a, out):
    table, at = constants()
    ctx = ExitStack()
    with ctx:
        def sb(name, shape, dt=F32):
            return ctx.enter_context(nc.sbuf_tensor(name, shape, dt))

        def scratch(name, shape, dt=F32):
            return nc.dram_tensor(name, shape, dt).ap()

        mod_dram = [scratch(f"mod_rows{l}", (2, 6 * D)) for l in range(DEPTH)]
        h2_dram = scratch("h2_rows", (NT * P, D))
        y_dram = scratch("expert_rows", (NBLK * P, D))

        CON = sb("CON", [P, table.shape[1]])
        X = sb("X", [P, NT, D])
        HT = sb("HT", [P, KD, NT * P])
        RING = sb("RING", [P, 6, KD * 512])
        WORK = sb("WORK", [P, 16448])
        small = sb("small", [P, 1100])
        meta = sb("meta", [P, NBLK + 1], I32)
        slot_tok = sb("slot_tok", [P, NBLK], U32)
        cur_tok = sb("cur_tok", [P, 2], U32)
        pos_u = sb("pos_u", [P, 2, NT], U32)
        pos_i = sb("pos_i", [P, 3, 2, NT], I32)
        bank = [ctx.enter_context(nc.psum_tensor(f"bank{i}", [P, 512], F32)) for i in range(8)]

        def con(name):
            o, n = at[name]
            return CON[:, o:o + n]

        ident = con("ident")

        def carve(base, start):
            pos = [start]

            def take(*shape):
                n = int(np.prod(shape))
                v = base[:, pos[0]:pos[0] + n]
                pos[0] += n
                assert pos[0] <= base.shape[1]
                if len(shape) == 2:
                    v = v.rearrange("p (a b) -> p a b", b=shape[1])
                elif len(shape) == 3:
                    v = v.rearrange("p (a b c) -> p a b c", b=shape[1], c=shape[2])
                return v
            return take

        tk = carve(small, 0)
        modT = tk(KD, 4)
        sT = tk(KD, 2)
        crow_T = tk(KD, 2)
        convT = tk(DEPTH, CONV * CHT)
        alog, dtb, nsink, rbias = tk(DEPTH, 8), tk(DEPTH, 8), tk(DEPTH, HB), tk(NE)
        gdn_g = tk(DEPTH, P)
        ss, rstd, st1, st2 = tk(16), tk(16), tk(16), tk(16)
        beta, gg, gcum, gtot = tk(NT, 8), tk(NT, 8), tk(NT, 8), tk(NT, 8)
        eg, egt, ek, nbg, nbeta, bt = tk(NT, 8), tk(NT, 8), tk(NT, 8), tk(NT, 8), tk(NT, 8), tk(NT, 8)
        mx, nm, den, esk = tk(NT, HB), tk(NT, HB), tk(NT, HB), tk(NT, HB)
        wkeep = tk(2, NT)

        slot45 = RING[:, SLOTS:6, :].rearrange("p a b -> p (a b)")

        tk = carve(WORK, 0)
        modrow = tk(6 * D)
        gnorm = tk(2, D)
        crow, cwrow = tk(P), tk(DEPTH, P)
        tk = carve(WORK, 10000)
        nsq, xn = tk(D), tk(2, D)
        tk = carve(WORK, 0)
        QK = tk(8, NT * P)
        krow, vrow = tk(NT, HA * P), tk(NT, HA * P)
        zrow = tk(NT, HA * P)
        arow = tk(NT, AROW)
        state = tk(2 * HA, P)
        orow = tk(NT, HA * P)
        tk = carve(slot45, 0)
        cpad, cy, vT, sq = tk(2, 2 * (SEQ + 4)), tk(2, 512), tk(4, 512), tk(2, 512)
        tk = carve(slot45, 0)
        gN, gNT, gY, gYT, gW, gE, gAt = ([tk(HA, P) for _ in range(2)] for _ in range(7))
        gsq = slot45[:, 0:NT * HA * P].rearrange("p (a b) -> p a b", b=P)
        tk = carve(slot45, 0)
        rtmp, kswap = tk(2, (HB + GB) * DH), tk(NT, P)
        qT, kTA, kTB = tk(NT, 4 * P), tk(NT * P), tk(NT * P)
        prob, probT = tk(2, 512), tk(2, 512)
        zero_tile = slot45[:, 7168:7168 + D]
        yb = QK[:, 0:4, :]
        yaT, ybT = QK[:, 4:8, :], krow
        mrow = WORK[:, 6144:6144 + NT * D].rearrange("p (t n) -> p t n", n=D)
        tk = carve(slot45, 0)
        ga, gb, pa, pb = tk(2, 512), tk(2, 512), tk(2, 512), tk(2, 512)
        g1bc = slot45[:, 4096:4096 + 2 * D].rearrange("p (s n) -> p s n", n=D)
        tk = carve(WORK, 0)
        h2, h2sq, h2T = tk(2, D), tk(D), tk(2, D)
        g2n, sh2bc = tk(2, D), tk(2, D)
        wr = tk(KD, NE)
        rt = [tk(NT, NE) for _ in range(14)]
        rg = [tk(NT, NG) for _ in range(5)]
        rp = tk(NT, NG, 6)
        r1 = [tk(NT) for _ in range(12)]
        wts = tk(2, NT)
        hot_r, hot_b = tk(2 * NT, P), tk(2 * NT, NBLK)
        re = [tk(NE) for _ in range(6)]
        cmpb, blk_e = tk(NBLK, NE), tk(NBLK + 1)
        tk = carve(WORK, 0)
        xg, xT, eg_s, he, heT, yrow = tk(2, D), tk(2, D), tk(2, FE), tk(2, FE), tk(2, FE), tk(2, D)
        tk = carve(WORK, 0)
        yg, g2bc, fg = tk(4, D), tk(2, D), tk(D)
        fsq = tk(D)

        PE_SIG = ["grow", "kk", "nt"] + [f"{x}{k}" for k in range(1, LV) for x in "wy"] + ["ks", "xr", "qs", "kv"]
        DV_SIG = ["gb", "clamp", "n", "attn", "lvl0"] + [f"{x}{k}" for k in range(1, LV) for x in "wy"] + ["r", "vs", "o", "state"]
        AC_SIG = ["exp", "nt", "vn"]

        per_layer = {
            "b_load": 96, "modmm": 12, "modev": 12, "modfold": 2, "modT_mm": 1, "modstore": 16, "bcload": 80,
            "rs0": 1, "xn": NT, "xt_mm": NT, "xt_ev": NT, "pj_mm": CHT, "pj_pad": CHT, "pj_conv": CHT, "pj_silu": CHT,
            "l2sq": 8, "l2mm": 8, "l2ln": 8, "l2out": 8, "tr_mm": 8, "tr_ev": 8, "row_mm": 3 * NT, "row_ev": 3 * NT,
            "gpre_a": 1, "gpre_d": 1, "gpre_mm": 1, "gpre_x": 1, "gpre_y": 1, "gpre_z": 1, "gpre_e": 1,
            "gp0": 4 * len(PE_SIG), "gp1": 4 * len(PE_SIG), "gd0": 4 * len(DV_SIG), "gd1": 4 * len(DV_SIG),
            "ga0": 4 * len(AC_SIG), "ga1": 4 * len(AC_SIG), "o_sq": 1, "o_rs": 1, "o_ya": 1, "rope": 1,
            "kt_mm": 1 + NT, "kt_ev": 1 + NT, "at_s": NT * HB, "at_nm": NT * HB, "at_p": NT * HB, "at_tr": NT * HB,
            "at_tev": NT * HB, "at_o": NT * HB, "at_y": NT, "mT_mm": 2 * NT, "mT_ev": 2 * NT, "mg_mm": 2 * NT,
            "mg_a": 2 * NT, "mg_d": 2 * NT, "m2_mm": 2 * NT, "m2_ev": 2 * NT, "y_mm": 2 * NT, "y_ev": 2 * NT,
            "g1load": 32, "n2rs0": 1, "h2row": NT, "h2st0": 32, "h2st1": 32, "r_tr": NT, "r_tev": NT, "r_mm": NT, "r_a": 1,
            "r_hot": 1, "r_rank": 1, "r_sort": 1, "r_inv": 1, "routed": 1, "g2load": 32, "comb": NT,
            "ygl0": 64, "ygl1": 64,
        }
        shared = {n: ctx.enter_context(nc.semaphore(n)) for n in per_layer}
        before = [{n: 0 for n in per_layer}, dict(per_layer)]
        looped = """xg_mm xg_ev0 xg_ev1 eg_mm eu_mm e_silu e_he ht_mm ht_ev ed_mm ed_ev0 ed_ev1 xgl0 xgl1 wl0 wl1 wl2 wl3 wl4 wl5 idx st0 st1""".split()
        S = [{**shared, **{n: ctx.enter_context(nc.semaphore(f"{n}_{l}")) for n in looped}} for l in range(DEPTH)]
        once = {n: ctx.enter_context(nc.semaphore(n)) for n in "c_T ct_mm c_silu params f_rs f_out".split()}
        ring_loaded = [ctx.enter_context(nc.semaphore(f"ring_loaded{s}")) for s in range(SLOTS)]
        x_loaded = ctx.enter_context(nc.semaphore("x_loaded"))
        con_loaded = ctx.enter_context(nc.semaphore("con_loaded"))
        small_loaded = ctx.enter_context(nc.semaphore("small_loaded"))
        zeroed = ctx.enter_context(nc.semaphore("zeroed"))
        fin_load = ctx.enter_context(nc.semaphore("fin_load"))
        stored = ctx.enter_context(nc.semaphore("stored"))
        dve_link = ctx.enter_context(nc.semaphore("dve_link"))
        act_link = ctx.enter_context(nc.semaphore("act_link"))
        y_zeroed = ctx.enter_context(nc.semaphore("y_zeroed"))
        pool_passed = ctx.enter_context(nc.semaphore("pool_passed"))
        pool_link = ctx.enter_context(nc.semaphore("pool_link"))

        def chunks(l):
            w_in = a["w_in"][l].rearrange("(k p) n -> p k n", p=P)
            w_mod = a["w_mod"][l].rearrange("(k p) n -> p k n", p=P)
            w_o = a["w_o"][l].rearrange("(k p) n -> p k n", p=P)
            oa = a["w_oa"][l].rearrange("(k p) n -> p k n", p=P)
            ob = a["w_ob"][l].rearrange("(k p) n -> p k n", p=P)
            for c in range(12):
                yield ("mod", c), [(0, 512, w_mod[:, :, 512 * c:512 * c + 512])]
            for c in range(5):
                yield ("in", c), [(0, 512, w_in[:, :, 512 * c:512 * c + 512])]
            yield ("in", 5), [(0, C_GA - 2560, w_in[:, :, 2560:C_GA])]
            for n in range(2):
                yield ("ga", n), [(0, 512, w_in[:, :, C_GA + 512 * n:C_GA + 512 * n + 512])]
                yield ("gb", n), [(0, 512, w_in[:, :, C_GB + 512 * n:C_GB + 512 * n + 512])]
                yield ("ab", n), [("lo", 512, oa[:, :, 512 * n:512 * n + 512]), ("hi", 512, ob[:, :, 512 * n:512 * n + 512])]
            for n in range(2):
                yield ("o", n), [(0, 512, w_o[:, :, 512 * n:512 * n + 512])]

        plan = [(l, key, parts) for l in range(DEPTH) for key, parts in chunks(l)]
        where = {(l, key): n for n, (l, key, _) in enumerate(plan)}
        fills = {}
        count = [0] * SLOTS
        for n, (l, key, parts) in enumerate(plan):
            count[n % SLOTS] += 16 * len(parts)
            fills[n] = count[n % SLOTS]
        first_of = [where[(l, ("mod", 0))] for l in range(DEPTH)] + [len(plan)]

        def ring(l, key):
            n = where[(l, key)]
            return RING[:, n % SLOTS, :].rearrange("p (k n) -> p k n", n=512)

        def ring_wait(pe, l, key):
            n = where[(l, key)]
            pe.wait_ge(ring_loaded[n % SLOTS], fills[n])

        def used(n):
            l, (kind, c), _ = plan[n]
            nact = len(active(l))
            if kind == "mod":
                name, v = "modmm", c + 1
            elif kind == "in" and c < 3:
                name, v = "pj_mm", 4 * (c + 1)
            elif kind == "in":
                name, v = "row_mm", sum(1 for q in range(3, c + 1) for _ in row_parts(l, q))
            else:
                name, v = ("y_mm" if kind == "o" else "mg_mm"), nact * (c + 1)
            return S[l][name], before[l][name] + v

        def active(l):
            return [0, 1, 2, 3] if l < DEPTH - 1 else [2, 3]

        def stream(t):
            return t // 2

        def bc(ap, *shape):
            return ap.to_broadcast([P, *shape])

        def per_row(v, t, c0, n):
            return v[:, t, c0:c0 + n].rearrange("p (h o) -> p h o", o=1).to_broadcast([P, n, P])

        def per_mat(m, n=HA):
            return m.rearrange("p (o j) -> p o j", o=1).to_broadcast([P, n, P])

        scan = [((0, 0), (1, 1)), ((0, 1), (1, 0)), ((0, 2), (1, 3)), ((0, 3), (1, 2))]
        def gv(sigs, g, name):
            return g * len(sigs) + sigs.index(name) + 1

        def row_parts(l, c):
            for t in range(NT):
                full = t in active(l)
                if c == 3:
                    if full:
                        yield t, (0, 512, 0)
                elif c == 4:
                    yield t, (0, 512 if full else 16, 0)
                else:
                    yield t, (0, 272, 512) if full else (16, 256, 528)

        def att_units(l):
            return [(j, t, h, 4 * P if t >= 2 else 2 * P, (5 - t) if t >= 2 else None)
                    for j, t in enumerate(active(l)) for h in range(HB)]

        def heads(bk):
            return bk[:, :].rearrange("p (h j) -> p h j", j=P)

        block = ctx.enter_context(nc.Block())

        @block.sync
        def _(sp):
            sp.dma_start(CON[:, :], a["table"]).then_inc(con_loaded, 16)
            sp.dma_start(crow[0:8, :], a["c_ctx"].rearrange("(k p) -> k p", p=P)).then_inc(small_loaded, 16)
            sp.dma_start(crow[8:16, :], a["c"].rearrange("o (k p) -> (o k) p", p=P)).then_inc(small_loaded, 16)
            for l in range(DEPTH):
                sp.dma_start(cwrow[0:CONV * CHT, l, :], a["conv_w"][l].rearrange("j (t p) -> (j t) p", p=P)).then_inc(small_loaded, 16)

            def load_chunk(n):
                l, key, parts = plan[n]
                if n - SLOTS >= first_of[l]:
                    sp.wait_ge(*used(n - SLOTS))
                for k0, width, src in parts:
                    dst = RING[:, n % SLOTS, :].rearrange("p (k n) -> p k n", n=512)
                    dst = dst[:, 4:8, :] if k0 == "hi" else dst[:, 0:4, :] if k0 == "lo" else dst[:, :, 0:width]
                    sp.dma_start(dst, src).then_inc(ring_loaded[n % SLOTS], 16)

            def layer(l):
                s, c0 = S[l], before[l]
                n0 = first_of[l]
                if l:
                    sp.wait_ge(S[l - 1]["comb"], before[l - 1]["comb"] + len(active(l - 1)))
                for r in range(2):
                    sp.dma_start(modrow[r:r + 1, :], a["b_mod"][l:l + 1, :]).then_inc(s["b_load"], 16)
                    for j, g in enumerate(("norm1_g", "norm2_g")):
                        sp.dma_start(gnorm[r:r + 1, j, :], a[g][l:l + 1, :]).then_inc(s["b_load"], 16)
                for n in range(n0, n0 + 12):
                    load_chunk(n)
                    if l == 0 and n == 3:
                        sp.dma_start(X[:, 0:2, :], a["ctx"].rearrange("o (t p) d -> p (o t) d", p=P)).then_inc(x_loaded, 16)
                        sp.dma_start(X[:, 2:4, :], a["x"].rearrange("o (t p) d -> p (o t) d", p=P)).then_inc(x_loaded, 16)
                for n in range(n0 + 12, first_of[l + 1]):
                    load_chunk(n)
                    if n == n0 + 19:
                        sp.wait_ge(s["modstore"], c0["modstore"] + 16)
                        sp.wait_ge(s["at_y"], c0["at_y"] + len(active(l)))
                        for st in range(2):
                            sp.dma_start(g1bc[:, st, :], mod_dram[l][st:st + 1, 2 * D:3 * D].to_broadcast([P, D])).then_inc(s["g1load"], 16)
                sp.wait_ge(s["m2_mm"], c0["m2_mm"] + len(active(l)) * 2)
                for st in range(2):
                    sp.dma_start(sh2bc[:, st, :], mod_dram[l][st:st + 1, 3 * D:4 * D].to_broadcast([P, D])).then_inc(s["bcload"], 16)
                    sp.dma_start(g2n[:, st, :], mod_dram[l][st:st + 1, 4 * D:5 * D].to_broadcast([P, D])).then_inc(s["bcload"], 16)
                sp.dma_start(wr, a["w_router"].rearrange("(k p) e -> p k e", p=P)).then_inc(s["bcload"], 16)

                sp.wait_ge(s["routed"], c0["routed"] + 1)
                sp.wait_ge(y_zeroed, 16)
                nblk = sp.value_load(meta[0:1, NBLK:NBLK + 1], min_val=1, max_val=NBLK)
                with sp.Fori(0, NBLK // 2) as i:
                    for u in range(2):
                        b = i * 2 + u
                        with sp.If(b < nblk):
                            e = sp.value_load(meta[0:1, bass.ds(b, 1)], min_val=0, max_val=NE - 1)
                            for j, w in enumerate(("w_gate", "w_up", "w_down")):
                                dst = RING[:, 3 * u + j, :]
                                if j < 2:
                                    src = a[w][l, bass.ds(e, 1), :, :].rearrange("o (k p) n -> p (o k) n", p=P)
                                    dst = dst.rearrange("p (k n) -> p k n", n=FE)
                                else:
                                    src = a[w][l, bass.ds(e, 1), :, :].rearrange("o (k p) n -> p (o k) n", p=P)
                                    dst = dst.rearrange("p (k n) -> p k n", n=D)
                                sp.wait_ge(s[("eg_mm", "eu_mm", "ed_mm")[j]], b + 1)
                                sp.dma_start(dst, src).then_inc(s[f"wl{3 * u + j}"], 16)
                sp.wait_ge(s["ed_mm"], nblk + 2)
                for st in range(2):
                    sp.dma_start(g2bc[:, st, :], mod_dram[l][st:st + 1, 5 * D:6 * D].to_broadcast([P, D])).then_inc(s["g2load"], 16)
                if l == DEPTH - 1:
                    sp.dma_start(fg, a["final_g"].rearrange("(o n) -> o n", o=1).to_broadcast([P, D])).then_inc(fin_load, 16)

            for l in range(DEPTH):
                layer(l)
            sp.wait_ge(stored, 32)

        @block.gpsimd
        def _(pool):
            for l in range(DEPTH):
                row = lambda x, n: x.rearrange("(o n) -> o n", o=1).to_broadcast([P, n])
                pool.dma_start(alog[:, l, :], row(a["a_log"][l].rearrange("d h -> (d h)"), 8)).then_inc(once["params"], 16)
                pool.dma_start(dtb[:, l, :], row(a["dt_bias"][l].rearrange("d h -> (d h)"), 8)).then_inc(once["params"], 16)
                pool.dma_start(nsink[:, l, :], row(a["sink"][l], HB)).then_inc(once["params"], 16)
                pool.dma_start(gdn_g[:, l, :], row(a["gdn_norm_g"][l], P)).then_inc(once["params"], 16)
            pool.dma_start(rbias, a["router_bias"].rearrange("(o n) -> o n", o=1).to_broadcast([P, NE])).then_inc(once["params"], 16)
            pool.memset(zero_tile, 0.0).then_inc(pool_link, 1)
            for l in range(DEPTH):
                s, c0 = S[l], before[l]
                pool.wait_ge(s["modfold"], c0["modfold"] + 2)
                pool.dma_start(mod_dram[l], modrow[0:2, :]).then_inc(s["modstore"], 16)
                if l == 0:
                    pool.wait_ge(pool_link, 1)
                    pool.wait_ge(s["gpre_a"], c0["gpre_a"] + 1)
                    pool.dma_start(y_dram.rearrange("(b p) d -> p b d", p=P),
                                   zero_tile.rearrange("p (o d) -> p o d", o=1).to_broadcast([P, NBLK, D])).then_inc(y_zeroed, 16)
                nact = len(active(l))
                for j, t in enumerate(active(l)):
                    pool.wait_ge(s["h2row"], c0["h2row"] + j + 1)
                    pool.dma_start(h2_dram[t * P:(t + 1) * P, :], h2[:, j % 2, :]).then_inc(s[f"h2st{j % 2}"], 16)
                pool.wait_ge(s["h2st0"], c0["h2st0"] + 8 * nact)
                pool.wait_ge(s["h2st1"], c0["h2st1"] + 8 * nact)
                pool.wait_ge(s["routed"], c0["routed"] + 1)
                nblk = pool.value_load(meta[0:1, NBLK:NBLK + 1], min_val=1, max_val=NBLK)
                with pool.Fori(0, NBLK // 2) as i:
                    for u in range(2):
                        b = i * 2 + u
                        with pool.If(b < nblk):
                            pool.wait_ge(s["xg_mm"], b + 1)
                            pool.wait_ge(s["routed"], c0["routed"] + 1)
                            pool.tensor_copy(cur_tok[:, u:u + 1], slot_tok[:, bass.ds(b, 1)]).then_inc(s["idx"], 1)
                            pool.wait_ge(s["idx"], b + 1)
                            pool.sem_inc(pool_passed, 1)
                            pool.indirect_dma_start(xg[:, u, :], None, h2_dram,
                                                    bass.IndirectOffsetOnAxis(cur_tok[:, u:u + 1], 0)).then_inc(s[f"xgl{u}"], 16)
                pool.wait_ge(s["ed_mm"], nblk + 2)
                pool.wait_ge(s["st0"], (nblk + 1) // 2 * 16 + 16)
                pool.wait_ge(s["st1"], nblk // 2 * 16 + 16)
                pool.sem_inc(pool_passed, 1)
                for j, t in enumerate(active(l)):
                    if j >= 2:
                        pool.wait_ge(s["comb"], c0["comb"] + j - 1)
                    for c in range(2):
                        pool.indirect_dma_start(yg[:, 2 * (j % 2) + c, :], None, y_dram,
                                                bass.IndirectOffsetOnAxis(pos_u[:, c, t:t + 1], 0)).then_inc(s[f"ygl{j % 2}"], 16)

        @block.tensor
        def _(pe):
            def layer(l):
                s, c0 = S[l], before[l]
                act_t = active(l)
                if l == 0:
                    pe.wait_ge(con_loaded, 16)
                    pe.wait_ge(small_loaded, 16 * (2 + DEPTH))
                    pe.transpose(bank[0][:, 0:16], crow[0:16, :], ident[0:16, 0:16])
                    for m in range(DEPTH):
                        mm = pe.transpose(bank[1][:, 64 * m:64 * m + 60], cwrow[0:60, m, :], ident[0:60, 0:60])
                    mm.then_inc(once["ct_mm"], 1)
                pe.wait_ge(once["c_silu"], 1)
                for c in range(12):
                    ring_wait(pe, l, ("mod", c))
                    if c >= 4:
                        pe.wait_ge(s["modev"], c0["modev"] + c - 3)
                    elif l == 0:
                        pe.wait_ge(once["ct_mm"], 1)
                    w = ring(l, ("mod", c))
                    for k in range(KD):
                        mm = pe.matmul(bank[2 + c % 4][0:2, :], sT[:, k, :], w[:, k, :], start=k == 0, stop=k == KD - 1)
                    mm.then_inc(s["modmm"], 1)
                pe.wait_ge(s["modfold"], c0["modfold"] + 2)
                for k in range(KD):
                    for j in range(2):
                        mm = pe.matmul(bank[0][:, 4 * k + 2 * j:4 * k + 2 * j + 2], modrow[0:2, j * D + k * P:j * D + (k + 1) * P],
                                       ident[0:2, 0:2], start=True, stop=True)
                mm.then_inc(s["modT_mm"], 1)
                for t in range(NT):
                    pe.wait_ge(s["xn"], c0["xn"] + t + 1)
                    if t >= 2:
                        pe.wait_ge(s["xt_ev"], c0["xt_ev"] + t - 1)
                    for k in range(KD):
                        mm = pe.transpose(bank[2 + 2 * (t % 2) + k // 4][:, (k % 4) * P:(k % 4 + 1) * P],
                                          xn[:, t % 2, k * P:(k + 1) * P], ident)
                    mm.then_inc(s["xt_mm"], 1)
                pe.wait_ge(s["xt_ev"], c0["xt_ev"] + NT)
                for c in range(CHT):
                    if c % 4 == 0:
                        ring_wait(pe, l, ("in", c // 4))
                    if c >= 2:
                        pe.wait_ge(s["pj_pad"], c0["pj_pad"] + c - 1)
                    w = ring(l, ("in", c // 4))
                    for k in range(KD):
                        mm = pe.matmul(bank[c % 2][:, :], w[:, k, (c % 4) * P:(c % 4 + 1) * P], HT[:, k, :],
                                       start=k == 0, stop=k == KD - 1)
                    mm.then_inc(s["pj_mm"], 1)
                n = 0
                for c in range(3, 6):
                    ring_wait(pe, l, ("in", c))
                    w = ring(l, ("in", c))
                    for t, (o, width, _) in row_parts(l, c):
                        if n >= 2:
                            pe.wait_ge(s["row_ev"], c0["row_ev"] + n - 1)
                        for k in range(KD):
                            mm = pe.matmul(bank[2 + n % 2][:, 0:width], HT[:, k, t * P:(t + 1) * P], w[:, k, o:o + width],
                                           start=k == 0, stop=k == KD - 1)
                        mm.then_inc(s["row_mm"], 1)
                        n += 1
                for h in range(HA):
                    pe.wait_ge(s["pj_silu"], c0["pj_silu"] + 8 + h + 1)
                    transpose_rows(s, c0, h, vT[:, h, :], h)
                for c in range(8):
                    pe.wait_ge(s["l2sq"], c0["l2sq"] + c + 1)
                    if c >= 2:
                        pe.wait_ge(s["l2ln"], c0["l2ln"] + c - 1)
                    pe.matmul(bank[4 + c % 2][:, :], con("ones"), sq[:, c % 2, :], start=True, stop=True).then_inc(s["l2mm"], 1)
                for h in range(HA):
                    pe.wait_ge(s["l2out"], c0["l2out"] + 4 + h + 1)
                    transpose_rows(s, c0, 4 + h, QK[:, 4 + h, :], h)
                pe.wait_ge(s["gpre_d"], c0["gpre_d"] + 1)
                for t in range(NT):
                    pe.matmul(bank[2][:, t * 8:t * 8 + 4], con("upper"), gg[:, t, 0:4], start=True, stop=True)
                    pe.matmul(bank[2][:, t * 8 + 4:t * 8 + 8], con("lower"), gg[:, t, 4:8], start=True, stop=True)
                    mm = pe.matmul(bank[3][:, t * 8:t * 8 + 8], con("ones"), gg[:, t, :], start=True, stop=True)
                mm.then_inc(s["gpre_mm"], 1)
                pe.wait_ge(s["gpre_a"], c0["gpre_a"] + 1)
                pe.wait_ge(s["tr_ev"], c0["tr_ev"] + 8)
                for g, pair in enumerate(scan):
                    gdn_group(s, c0, g, pair)
                attention(l, s, c0)
                merge(l, s, c0)
                route(l, s, c0)
                experts(l, s, c0)

            def transpose_rows(s, c0, n, src, h):
                if n >= 2:
                    pe.wait_ge(s["tr_ev"], c0["tr_ev"] + n - 1)
                for t in range(NT):
                    mm = pe.transpose(bank[6 + n % 2][:, t * P:(t + 1) * P], src[:, t * P:(t + 1) * P], ident)
                mm.then_inc(s["tr_mm"], 1)

            def gdn_group(s, c0, g, pair):
                def each(f):
                    for d, t in pair:
                        f(d, t, slice(t * P, (t + 1) * P), bank[4 * d:4 * d + 4])

                def grow(d, t, ts, bk):
                    pe.wait_ge(s[f"gd{d}"], c0[f"gd{d}"] + gv(DV_SIG, g, "gb"))
                    for h in range(HA):
                        mm = pe.matmul(bk[0][:, h * P:(h + 1) * P], gW[d][:, h, :], con("lower" if d else "upper"), start=True, stop=True)
                    mm.then_inc(s[f"gp{d}"], 1)

                def kk(d, t, ts, bk):
                    for h in range(HA):
                        pe.matmul(bk[1][:, h * P:(h + 1) * P], QK[:, 4 + h, ts], QK[:, 4 + h, ts], start=True, stop=True)
                        mm = pe.matmul(bk[2][:, h * P:(h + 1) * P], QK[:, 4 + h, ts], QK[:, h, ts], start=True, stop=True)
                    mm.then_inc(s[f"gp{d}"], 1)

                def nt(d, t, ts, bk):
                    pe.wait_ge(s[f"gd{d}"], c0[f"gd{d}"] + gv(DV_SIG, g, "n"))
                    for h in range(HA):
                        mm = pe.transpose(bk[3][:, h * P:(h + 1) * P], gN[d][:, h, :], ident)
                    mm.then_inc(s[f"gp{d}"], 1)

                each(grow)
                each(kk)
                each(nt)
                for k in range(1, LV):
                    def w(d, t, ts, bk):
                        pe.wait_ge(s[f"gd{d}"], c0[f"gd{d}"] + gv(DV_SIG, g, "lvl0" if k == 1 else f"y{k - 1}"))
                        lt = gN[d] if d else gNT[d]
                        for h in range(HA):
                            mm = pe.matmul(bk[0][:, h * P:(h + 1) * P], lt[:, h, :], gY[d][:, h, :], start=True, stop=True)
                        mm.then_inc(s[f"gp{d}"], 1)

                    def y(d, t, ts, bk):
                        pe.wait_ge(s[f"gd{d}"], c0[f"gd{d}"] + gv(DV_SIG, g, f"w{k}"))
                        for h in range(HA):
                            if k < LV - 1 or d:
                                mm = pe.matmul(bk[1][:, h * P:(h + 1) * P], gYT[d][:, h, :], gW[d][:, h, :], start=True, stop=True)
                            if k < LV - 1 or not d:
                                mm = pe.matmul(bk[2][:, h * P:(h + 1) * P], gW[d][:, h, :], gYT[d][:, h, :], start=True, stop=True)
                        mm.then_inc(s[f"gp{d}"], 1)
                    each(w)
                    each(y)

                def ks(d, t, ts, bk):
                    if g:
                        pe.wait_ge(s[f"gd{d}"], c0[f"gd{d}"] + g * len(DV_SIG))
                    for h in range(HA):
                        mm = pe.matmul(bk[0][:, h * P:(h + 1) * P], QK[:, 4 + h, ts], state[:, 4 * d + h, :], start=True, stop=True)
                    mm.then_inc(s[f"gp{d}"], 1)

                def xr(d, t, ts, bk):
                    pe.wait_ge(s[f"gd{d}"], c0[f"gd{d}"] + gv(DV_SIG, g, "r"))
                    inv = gY[d] if d else gYT[d]
                    for h in range(HA):
                        mm = pe.matmul(bk[3][:, h * P:(h + 1) * P], inv[:, h, :], gN[d][:, h, :], start=True, stop=True)
                    mm.then_inc(s[f"gp{d}"], 1)

                def qs(d, t, ts, bk):
                    pe.wait_ge(s[f"ga{d}"], c0[f"ga{d}"] + gv(AC_SIG, g, "vn"))
                    for h in range(HA):
                        pe.matmul(bk[1][:, h * P:(h + 1) * P], QK[:, h, ts], state[:, 4 * d + h, :], start=True, stop=True)
                        mm = pe.matmul(bk[2][:, h * P:(h + 1) * P], gAt[d][:, h, :], gNT[d][:, h, :], start=True, stop=True)
                    mm.then_inc(s[f"gp{d}"], 1)

                def kv(d, t, ts, bk):
                    pe.wait_ge(s[f"gd{d}"], c0[f"gd{d}"] + gv(DV_SIG, g, "vs"))
                    for h in range(HA):
                        mm = pe.matmul(bk[0][:, h * P:(h + 1) * P], krow[:, t, h * P:(h + 1) * P], gE[d][:, h, :], start=True, stop=True)
                    mm.then_inc(s[f"gp{d}"], 1)
                each(ks)
                each(xr)
                each(qs)
                each(kv)

            def attention(l, s, c0):
                pe.wait_ge(s["rope"], c0["rope"] + 1)
                for d in range(2):
                    pe.wait_ge(s[f"gd{d}"], c0[f"gd{d}"] + len(scan) * len(DV_SIG))
                for t in range(NT):
                    pe.transpose(bank[0][:, t * P:(t + 1) * P], arow[:, t, A_K:A_K + P], ident)
                    mm = pe.transpose(bank[1][:, t * P:(t + 1) * P], kswap[:, t, :], ident)
                mm.then_inc(s["kt_mm"], 1)
                for j, t in enumerate(active(l)):
                    for m in range(4):
                        mm = pe.transpose(bank[2 + j][:, m * P:(m + 1) * P], arow[:, t, A_Q + m * P:A_Q + (m + 1) * P], ident)
                    mm.then_inc(s["kt_mm"], 1)
                pe.wait_ge(s["kt_ev"], c0["kt_ev"] + 1 + len(active(l)))
                units = att_units(l)
                for n in range(len(units) + 1):
                    if n < len(units):
                        j, t, h, keys, _ = units[n]
                        if n >= 2:
                            pe.wait_ge(s["at_p"], c0["at_p"] + n - 1)
                        o, g = h % 2, h // (HB // GB)
                        kt = kTA if g == o else kTB
                        rows = slice(64 * o, 64 * o + 64)
                        pe.matmul(bank[n % 2][:, 0:keys], qT[rows, t, (h // 2) * P:(h // 2 + 1) * P], kt[rows, 0:keys],
                                  start=True, stop=True).then_inc(s["at_s"], 1)
                    if n >= 1:
                        j, t, h, keys, _ = units[n - 1]
                        pe.wait_ge(s["at_p"], c0["at_p"] + n)
                        if n >= 3:
                            pe.wait_ge(s["at_tev"], c0["at_tev"] + n - 2)
                        nk = keys // P
                        for q in range(nk):
                            mm = pe.transpose(bank[2 + (n - 1) % 2][:, q * P:(q + 1) * P], prob[:, (n - 1) % 2, q * P:(q + 1) * P], ident)
                        mm.then_inc(s["at_tr"], 1)
                        pe.wait_ge(s["at_tev"], c0["at_tev"] + n)
                        if h == 0 and j >= 2:
                            pe.wait_ge(s["at_y"], c0["at_y"] + j - 1)
                        for q in range(nk):
                            mm = pe.matmul(bank[4 + j % 2][:, h * DH:(h + 1) * DH], probT[:, (n - 1) % 2, q * P:(q + 1) * P],
                                           arow[:, q, A_V + (h // 4) * DH:A_V + (h // 4 + 1) * DH], start=q == 0, stop=q == nk - 1)
                        mm.then_inc(s["at_o"], 1)

            def merge(l, s, c0):
                act_t = active(l)
                n = 0
                for src, sem in ((orow, "o_ya"), (yb, "at_y")):
                    pe.wait_ge(s[sem], 1 if sem == "o_ya" else len(act_t))
                    for t in act_t:
                        if n >= 2:
                            pe.wait_ge(s["mT_ev"], c0["mT_ev"] + n - 1)
                        for k in range(4):
                            mm = pe.transpose(bank[6 + n % 2][:, k * P:(k + 1) * P], src[:, t, k * P:(k + 1) * P], ident)
                        mm.then_inc(s["mT_mm"], 1)
                        n += 1
                pe.wait_ge(s["mT_ev"], c0["mT_ev"] + n)
                n = 0
                for half in range(2):
                    for key in ("ga", "gb", "ab"):
                        ring_wait(pe, l, (key, half))
                    wa, wb, wab = (ring(l, (key, half)) for key in ("ga", "gb", "ab"))
                    for t in act_t:
                        ts = slice(t * P, (t + 1) * P)
                        bk = bank[4 * (n % 2):4 * (n % 2) + 4]
                        if n >= 2:
                            pe.wait_ge(s["mg_d"], c0["mg_d"] + n - 1)
                        for k in range(KD):
                            pe.matmul(bk[0][:, :], HT[:, k, ts], wa[:, k, :], start=k == 0, stop=k == KD - 1)
                        for k in range(KD):
                            pe.matmul(bk[1][:, :], HT[:, k, ts], wb[:, k, :], start=k == 0, stop=k == KD - 1)
                        for k in range(4):
                            pe.matmul(bk[2][:, :], yaT[:, k, ts], wab[:, k, :], start=k == 0, stop=k == 3)
                        for k in range(4):
                            mm = pe.matmul(bk[3][:, :], ybT[:, k, ts], wab[:, 4 + k, :], start=k == 0, stop=k == 3)
                        mm.then_inc(s["mg_mm"], 1)
                        n += 1
                pe.wait_ge(s["mg_d"], c0["mg_d"] + n)
                for j, t in enumerate(act_t):
                    if j >= 2:
                        pe.wait_ge(s["m2_ev"], c0["m2_ev"] + 2 * (j - 1))
                    for k in range(KD):
                        mm = pe.transpose(bank[2 * (j % 2) + k // 4][:, (k % 4) * P:(k % 4 + 1) * P], mrow[:, t, k * P:(k + 1) * P], ident)
                        if k % 4 == 3:
                            mm.then_inc(s["m2_mm"], 1)
                pe.wait_ge(s["m2_ev"], c0["m2_ev"] + 2 * len(act_t))
                n = 0
                for half in range(2):
                    ring_wait(pe, l, ("o", half))
                    w = ring(l, ("o", half))
                    for t in act_t:
                        if n >= 2:
                            pe.wait_ge(s["y_ev"], c0["y_ev"] + n - 1)
                        for k in range(KD):
                            mm = pe.matmul(bank[4 + n % 2][:, :], HT[:, k, t * P:(t + 1) * P], w[:, k, :], start=k == 0, stop=k == KD - 1)
                        mm.then_inc(s["y_mm"], 1)
                        n += 1

            def route(l, s, c0):
                act_t = active(l)
                pe.wait_ge(s["bcload"], c0["bcload"] + 80)
                for j, t in enumerate(act_t):
                    pe.wait_ge(s["h2row"], c0["h2row"] + j + 1)
                    if j >= 1:
                        pe.wait_ge(s["r_tev"], c0["r_tev"] + j)
                    for k in range(KD):
                        mm = pe.transpose(bank[k // 4][:, (k % 4) * P:(k % 4 + 1) * P], h2[:, j % 2, k * P:(k + 1) * P], ident)
                    mm.then_inc(s["r_tr"], 1)
                    pe.wait_ge(s["r_tev"], c0["r_tev"] + j + 1)
                    for k in range(KD):
                        mm = pe.matmul(bank[2][:, j * NE:(j + 1) * NE], h2T[:, j % 2, k * P:(k + 1) * P], wr[:, k, :],
                                       start=k == 0, stop=k == KD - 1)
                    mm.then_inc(s["r_mm"], 1)
                pe.wait_ge(s["r_hot"], c0["r_hot"] + 1)
                nact = len(act_t)
                hot = rt[5]
                for j in range(nact):
                    o = bank[3][:, j * NE:(j + 1) * NE]
                    for q in range(j):
                        pe.matmul(o, con("ones"), hot[:, q, :], start=q == 0, stop=False)
                    pe.matmul(o, con("supper"), hot[:, j, :], start=j == 0, stop=True)
                for q in range(nact):
                    mm = pe.matmul(bank[4][:, 0:NE], con("ones"), hot[:, q, :], start=q == 0, stop=q == nact - 1)
                mm.then_inc(s["r_rank"], 1)
                pe.wait_ge(s["r_sort"], c0["r_sort"] + 1)
                for q in range(2 * nact):
                    mm = pe.matmul(bank[5][:, 0:NBLK], hot_r[:, q, :], hot_b[:, q, :], start=q == 0, stop=q == 2 * nact - 1)
                mm.then_inc(s["r_inv"], 1)

            def experts(l, s, c0):
                pe.wait_ge(s["routed"], c0["routed"] + 1)
                nblk = pe.value_load(meta[0:1, NBLK:NBLK + 1], min_val=1, max_val=NBLK)
                for name in ("xg_mm", "eg_mm", "eu_mm", "ed_mm"):
                    pe.sem_inc(s[name], 2)
                with pe.Fori(0, NBLK // 2) as i:
                    for u in range(2):
                        b = i * 2 + u
                        with pe.If(b < nblk):
                            wg = RING[:, 3 * u, :].rearrange("p (k n) -> p k n", n=FE)
                            wu = RING[:, 3 * u + 1, :].rearrange("p (k n) -> p k n", n=FE)
                            wd = RING[:, 3 * u + 2, :].rearrange("p (k n) -> p k n", n=D)
                            pe.wait_ge(s[f"xgl{u}"], (i + 1) * 16)
                            for k in range(KD):
                                mm = pe.transpose(bank[k // 4][:, (k % 4) * P:(k % 4 + 1) * P], xg[:, u, k * P:(k + 1) * P], ident)
                            mm.then_inc(s["xg_mm"], 1)
                            pe.wait_ge(s["xg_ev0"], b + 1)
                            pe.wait_ge(s["xg_ev1"], b + 1)
                            pe.wait_ge(s[f"wl{3 * u}"], (i + 1) * 16)
                            for k in range(KD):
                                mm = pe.matmul(bank[2][:, :], xT[:, u, k * P:(k + 1) * P], wg[:, k, :], start=k == 0, stop=k == KD - 1)
                            mm.then_inc(s["eg_mm"], 1)
                            pe.wait_ge(s[f"wl{3 * u + 1}"], (i + 1) * 16)
                            for k in range(KD):
                                mm = pe.matmul(bank[3][:, :], xT[:, u, k * P:(k + 1) * P], wu[:, k, :], start=k == 0, stop=k == KD - 1)
                            mm.then_inc(s["eu_mm"], 1)
                            pe.wait_ge(s["e_he"], b + 1)
                            for k in range(KF):
                                mm = pe.transpose(bank[4][:, k * P:(k + 1) * P], he[:, u, k * P:(k + 1) * P], ident)
                            mm.then_inc(s["ht_mm"], 1)
                            pe.wait_ge(s["ht_ev"], b + 1)
                            pe.wait_ge(s["ed_ev0"], b + 1)
                            pe.wait_ge(s["ed_ev1"], b + 1)
                            pe.wait_ge(s[f"wl{3 * u + 2}"], (i + 1) * 16)
                            for n in range(2):
                                for k in range(KF):
                                    mm = pe.matmul(bank[5 + n][:, :], heT[:, u, k * P:(k + 1) * P], wd[:, k, n * 512:(n + 1) * 512],
                                                   start=k == 0, stop=k == KF - 1)
                            mm.then_inc(s["ed_mm"], 1)

            for l in range(DEPTH):
                layer(l)

        @block.scalar
        def _(act):
            n_link = [0]

            def link(ins):
                n_link[0] += 1
                ins.then_inc(act_link, 1)
                act.wait_ge(act_link, n_link[0])

            def layer(l):
                s, c0 = S[l], before[l]
                act_t = active(l)
                if l == 0:
                    act.wait_ge(once["c_T"], 1)
                    act.activation(sT[:, :, :], crow_T[:, :, :], ACT.Silu).then_inc(once["c_silu"], 1)
                if l == 0:
                    act.wait_ge(x_loaded, 32)
                else:
                    act.wait_ge(S[l - 1]["comb"], before[l - 1]["comb"] + len(active(l - 1)))
                for t in range(NT):
                    link(act.activation(nsq, X[:, t, :], ACT.Square, accum_out=ss[:, t:t + 1]))
                link(act.activation(st1[:, 0:NT], ss[:, 0:NT], ACT.Ln, scale=1.0 / D, bias=con("eps")))
                act.activation(rstd[:, 0:NT], st1[:, 0:NT], ACT.Exp, scale=-0.5).then_inc(s["rs0"], 1)
                for c in range(CHT + 1):
                    if c < CHT:
                        act.wait_ge(s["pj_mm"], c0["pj_mm"] + c + 1)
                        act.wait_ge(zeroed, l + 1) if c == 0 else None
                        if c >= 2:
                            act.wait_ge(s["pj_conv"], c0["pj_conv"] + c - 1)
                        dst = cpad[:, c % 2, :].rearrange("p (s n) -> p s n", s=2)[:, :, 2:2 + SEQ]
                        act.copy(dst, bank[c % 2][:, :].rearrange("p (s n) -> p s n", s=2)).then_inc(s["pj_pad"], 1)
                    if c >= 1:
                        d = c - 1
                        act.wait_ge(s["pj_conv"], c0["pj_conv"] + d + 1)
                        if d == 0:
                            act.wait_ge(s["modstore"], c0["modstore"] + 16)
                        dst = QK[:, d, :] if d < 8 else vT[:, d - 8, :]
                        act.activation(dst, cy[:, d % 2, :], ACT.Silu).then_inc(s["pj_silu"], 1)
                n = 0
                for c in range(3, 6):
                    for t, (o, width, dcol) in row_parts(l, c):
                        act.wait_ge(s["row_mm"], c0["row_mm"] + n + 1)
                        if c == 3:
                            act.activation(zrow[:, t, :], bank[2 + n % 2][:, 0:512], ACT.Silu).then_inc(s["row_ev"], 1)
                        else:
                            act.copy(arow[:, t, dcol:dcol + width], bank[2 + n % 2][:, 0:width]).then_inc(s["row_ev"], 1)
                        n += 1
                act.wait_ge(s["pj_silu"], c0["pj_silu"] + 12)
                for c in range(8):
                    if c >= 2:
                        act.wait_ge(s["l2mm"], c0["l2mm"] + c - 1)
                    act.activation(sq[:, c % 2, :], QK[:, c, :], ACT.Square).then_inc(s["l2sq"], 1)
                    if c >= 1:
                        l2_rs(s, c0, c - 1)
                l2_rs(s, c0, 7)
                act.wait_ge(s["row_ev"], c0["row_ev"] + n)
                pass
                link(act.activation(bt[:, :, :], arow[:, :, 0:8], ACT.Exp, scale=-1.0))
                act.wait_ge(once["params"], 16 * (4 * DEPTH + 1))
                link(act.activation(nbeta[:, 0, :], alog[:, l, :], ACT.Exp))
                act.wait_ge(s["gpre_x"], c0["gpre_x"] + 1)
                link(act.activation(gcum[:, :, :], gcum[:, :, :], ACT.Exp, scale=-1.0))
                act.activation(gcum[:, :, :], gcum[:, :, :], ACT.Ln, bias=1.0).then_inc(s["gpre_y"], 1)
                act.wait_ge(s["gpre_z"], c0["gpre_z"] + 1)
                act.activation(eg[:, :, :], gcum[:, :, :], ACT.Exp)
                act.activation(egt[:, :, :], gtot[:, :, :], ACT.Exp)
                act.activation(ek[:, :, :], ek[:, :, :], ACT.Exp).then_inc(s["gpre_e"], 1)
                for g, pair in enumerate(scan):
                    for d, t in pair:
                        act.wait_ge(s[f"gd{d}"], c0[f"gd{d}"] + gv(DV_SIG, g, "clamp"))
                        act.activation(gE[d][:, :, :], gE[d][:, :, :], ACT.Exp, scale=-1.0)
                        act.activation(gAt[d][:, :, :], gAt[d][:, :, :], ACT.Exp).then_inc(s[f"ga{d}"], 1)
                    for d, t in pair:
                        act.wait_ge(s[f"gp{d}"], c0[f"gp{d}"] + gv(PE_SIG, g, "nt"))
                        act.copy(gNT[d][:, :, :], heads(bank[4 * d + 3])).then_inc(s[f"ga{d}"], 1)
                    for d, t in pair:
                        act.wait_ge(s[f"gp{d}"], c0[f"gp{d}"] + gv(PE_SIG, g, "xr"))
                        act.copy(gNT[d][:, :, :], heads(bank[4 * d + 3])).then_inc(s[f"ga{d}"], 1)
                act.wait_ge(s["o_sq"], c0["o_sq"] + 1)
                nn = 4 * len(act_t)
                link(act.activation(st1[:, 0:nn], ss[:, 0:nn], ACT.Ln, scale=1.0 / P, bias=con("eps")))
                act.activation(rstd[:, 0:nn], st1[:, 0:nn], ACT.Exp, scale=-0.5).then_inc(s["o_rs"], 1)
                for n, (j, t, h, keys, _) in enumerate(att_units(l)):
                    act.wait_ge(s["at_nm"], c0["at_nm"] + n + 1)
                    if n >= 2:
                        act.wait_ge(s["at_tr"], c0["at_tr"] + n - 1)
                    act.activation(esk[:, t, h:h + 1], nsink[:, l, h:h + 1], ACT.Exp, scale=-1.0, bias=nm[:, t, h:h + 1])
                    act.activation(prob[:, n % 2, 0:keys], bank[n % 2][:, 0:keys], ACT.Exp, scale=SCALE, bias=nm[:, t, h:h + 1],
                                   accum_out=den[:, t, h:h + 1]).then_inc(s["at_p"], 1)
                n = 0
                for half in range(2):
                    for t in act_t:
                        act.wait_ge(s["mg_mm"], c0["mg_mm"] + n + 1)
                        if n >= 2:
                            act.wait_ge(s["mg_d"], c0["mg_d"] + n - 1)
                        bk = bank[4 * (n % 2):4 * (n % 2) + 4]
                        act.activation(ga[:, n % 2, :], bk[0][:, :], ACT.Exp, scale=-1.0)
                        act.activation(gb[:, n % 2, :], bk[1][:, :], ACT.Exp, scale=-1.0).then_inc(s["mg_a"], 1)
                        n += 1
                act.wait_ge(s["y_ev"], c0["y_ev"] + 2 * len(act_t))
                for j, t in enumerate(act_t):
                    link(act.activation(h2sq, X[:, t, :], ACT.Square, accum_out=ss[:, j:j + 1]))
                nn = len(act_t)
                link(act.activation(st1[:, 0:nn], ss[:, 0:nn], ACT.Ln, scale=1.0 / D, bias=con("eps")))
                act.activation(rstd[:, 0:nn], st1[:, 0:nn], ACT.Exp, scale=-0.5).then_inc(s["n2rs0"], 1)
                act.wait_ge(s["r_mm"], c0["r_mm"] + nn)
                act.activation(rt[0][:, 0:nn, :], bank[2][:, 0:nn * NE].rearrange("p (t e) -> p t e", e=NE), ACT.Exp,
                               scale=-1.0).then_inc(s["r_a"], 1)
                act.wait_ge(s["routed"], c0["routed"] + 1)
                act.wait_ge(y_zeroed, 16)
                nblk = act.value_load(meta[0:1, NBLK:NBLK + 1], min_val=1, max_val=NBLK)
                act.sem_inc(s["ed_ev1"], 1)
                act.sem_inc(s["st0"], 16)
                act.sem_inc(s["st1"], 16)
                with act.Fori(0, NBLK // 2) as i:
                    for u in range(2):
                        b = i * 2 + u
                        with act.If(b < nblk):
                            act.wait_ge(s["xg_mm"], b + 3)
                            act.copy(xT[:, u, 512:1024], bank[1][:, :]).then_inc(s["xg_ev1"], 1)
                            act.wait_ge(s["eg_mm"], b + 3)
                            act.activation(eg_s[:, u, :], bank[2][:, :], ACT.Silu).then_inc(s["e_silu"], 1)
                            act.wait_ge(s["ht_mm"], b + 1)
                            act.copy(heT[:, u, :], bank[4][:, :]).then_inc(s["ht_ev"], 1)
                            act.wait_ge(s[f"st{u}"], (i + 1) * 16)
                            act.wait_ge(s["ed_mm"], b + 3)
                            act.copy(yrow[:, u, 512:1024], bank[6][:, :]).then_inc(s["ed_ev1"], 1)
                            act.wait_ge(s["ed_ev1"], b + 2)
                            act.wait_ge(s["ed_ev0"], b + 2)
                            act.dma_start(y_dram[bass.ds(b * P, P), :], yrow[:, u, :]).then_inc(s[f"st{u}"], 16)
                if l == DEPTH - 1:
                    act.wait_ge(s["comb"], c0["comb"] + 2)
                    for j, t in enumerate(act_t):
                        link(act.activation(fsq, X[:, t, :], ACT.Square, accum_out=ss[:, j:j + 1]))
                    link(act.activation(st1[:, 0:2], ss[:, 0:2], ACT.Ln, scale=1.0 / D, bias=con("eps")))
                    act.activation(rstd[:, 0:2], st1[:, 0:2], ACT.Exp, scale=-0.5).then_inc(once["f_rs"], 1)
                    for j, t in enumerate(act_t):
                        act.wait_ge(once["f_out"], j + 1)
                        act.dma_start(out[0, j * P:(j + 1) * P, :], X[:, t, :]).then_inc(stored, 16)

            def l2_rs(s, c0, c):
                act.wait_ge(s["l2mm"], c0["l2mm"] + c + 1)
                if c >= 2:
                    act.wait_ge(s["l2out"], c0["l2out"] + c - 1)
                link(act.activation(cy[:, c % 2, :], bank[4 + c % 2][:, :], ACT.Ln, bias=con("eps")))
                act.activation(cy[:, c % 2, :], cy[:, c % 2, :], ACT.Exp, scale=-0.5).then_inc(s["l2ln"], 1)

            for l in range(DEPTH):
                layer(l)

        @block.vector
        def _(dve):
            n_link = [0]

            def link(ins):
                n_link[0] += 1
                ins.then_inc(dve_link, 1)
                dve.wait_ge(dve_link, n_link[0])

            def newton(n, inv_width):
                link(dve.tensor_scalar(st1[:, 0:n], ss[:, 0:n], inv_width, EPS, ALU.mult, ALU.add))
                link(dve.tensor_tensor(st2[:, 0:n], rstd[:, 0:n], rstd[:, 0:n], ALU.mult))
                link(dve.tensor_tensor(st2[:, 0:n], st2[:, 0:n], st1[:, 0:n], ALU.mult))
                link(dve.tensor_scalar(st2[:, 0:n], st2[:, 0:n], -0.5, 1.5, ALU.mult, ALU.add))
                link(dve.tensor_tensor(rstd[:, 0:n], rstd[:, 0:n], st2[:, 0:n], ALU.mult))

            def layer(l):
                s, c0 = S[l], before[l]
                act_t = active(l)
                if l == 0:
                    dve.wait_ge(once["ct_mm"], 1)
                    link(dve.tensor_copy(convT[:, 0, :], bank[1][:, 0:60]))
                    link(dve.tensor_copy(convT[:, 1, :], bank[1][:, 64:124]))
                    dve.tensor_copy(crow_T[:, :, :], bank[0][:, 0:16].rearrange("p (s k) -> p k s", s=2)).then_inc(once["c_T"], 1)
                    dve.wait_ge(once["params"], 16 * (4 * DEPTH + 1))
                    link(dve.tensor_scalar(nsink[:, :, :], nsink[:, :, :], -1.0, None, ALU.mult))
                dve.wait_ge(s["b_load"], c0["b_load"] + 96)
                for c in range(12):
                    dve.wait_ge(s["modmm"], c0["modmm"] + c + 1)
                    sl = modrow[0:2, 512 * c:512 * c + 512]
                    dve.tensor_tensor(sl, bank[2 + c % 4][0:2, :], sl, ALU.add).then_inc(s["modev"], 1)
                dve.wait_ge(s["modev"], c0["modev"] + 12)
                for j, c in enumerate((1, 4)):
                    sl = modrow[0:2, c * D:(c + 1) * D]
                    dve.scalar_tensor_tensor(out=sl, in0=sl, scalar=1.0, in1=gnorm[0:2, j, :], op0=ALU.add, op1=ALU.mult).then_inc(s["modfold"], 1)
                dve.wait_ge(s["modT_mm"], c0["modT_mm"] + 1)
                link(dve.tensor_copy(modT[:, :, :], bank[0][:, 0:32].rearrange("p (k m) -> p k m", m=4)))
                dve.wait_ge(s["rs0"], c0["rs0"] + 1)
                newton(NT, 1.0 / D)
                for t in range(NT + 1):
                    if t < NT:
                        if t >= 2:
                            dve.wait_ge(s["xt_mm"], c0["xt_mm"] + t - 1)
                        dve.tensor_scalar(xn[:, t % 2, :], X[:, t, :], rstd[:, t:t + 1], None, ALU.mult).then_inc(s["xn"], 1)
                    if t >= 1:
                        q = t - 1
                        dve.wait_ge(s["xt_mm"], c0["xt_mm"] + q + 1)
                        for k in range(KD):
                            last = dve.tensor_scalar(HT[:, k, q * P:(q + 1) * P], bank[2 + 2 * (q % 2) + k // 4][:, (k % 4) * P:(k % 4 + 1) * P],
                                                     modT[:, k, 2 + stream(q):3 + stream(q)], modT[:, k, stream(q):stream(q) + 1],
                                                     ALU.mult, ALU.add)
                        last.then_inc(s["xt_ev"], 1)
                dve.memset(cpad[:, :, :], 0.0).then_inc(zeroed, 1)
                for c in range(CHT):
                    dve.wait_ge(s["pj_pad"], c0["pj_pad"] + c + 1)
                    if c >= 2:
                        dve.wait_ge(s["pj_silu"], c0["pj_silu"] + c - 1)
                    src = cpad[:, c % 2, :].rearrange("p (s n) -> p s n", s=2)
                    dst = cy[:, c % 2, :].rearrange("p (s n) -> p s n", s=2)
                    link(dve.tensor_scalar(dst, src[:, :, 0:SEQ], convT[:, l, c:c + 1], None, ALU.mult))
                    for j in range(1, CONV):
                        ins = dve.scalar_tensor_tensor(out=dst, in0=src[:, :, j:j + SEQ], scalar=convT[:, l, j * CHT + c:j * CHT + c + 1],
                                                       in1=dst, op0=ALU.mult, op1=ALU.add)
                        if j < CONV - 1:
                            link(ins)
                        else:
                            ins.then_inc(s["pj_conv"], 1)
                for h in range(HA):
                    dve.wait_ge(s["tr_mm"], c0["tr_mm"] + h + 1)
                    dve.tensor_copy(vrow[:, :, h * P:(h + 1) * P], bank[6 + h % 2][:, :].rearrange("p (t j) -> p t j", j=P)).then_inc(s["tr_ev"], 1)
                for c in range(8):
                    dve.wait_ge(s["l2ln"], c0["l2ln"] + c + 1)
                    dve.scalar_tensor_tensor(out=QK[:, c, :], in0=QK[:, c, :], scalar=float(P) ** -0.5 if c < 4 else 1.0,
                                             in1=cy[:, c % 2, :], op0=ALU.mult, op1=ALU.mult).then_inc(s["l2out"], 1)
                for h in range(HA):
                    dve.wait_ge(s["tr_mm"], c0["tr_mm"] + 4 + h + 1)
                    dve.tensor_copy(krow[:, :, h * P:(h + 1) * P], bank[6 + h % 2][:, :].rearrange("p (t j) -> p t j", j=P)).then_inc(s["tr_ev"], 1)
                dve.wait_ge(s["row_ev"], c0["row_ev"] + sum(1 for c in range(3, 6) for _ in row_parts(l, c)))
                per_tile = lambda v: v[:, l, :].rearrange("p (o h) -> p o h", o=1).to_broadcast([P, NT, 8])
                link(dve.tensor_tensor(gg[:, :, :], arow[:, :, 8:16], per_tile(dtb), ALU.add))
                link(dve.tensor_scalar(gtot[:, :, :], gg[:, :, :], -1.0, None, ALU.mult))
                dve.tensor_tensor(gcum[:, :, :], gg[:, :, :], gtot[:, :, :], ALU.max).then_inc(s["gpre_x"], 1)
                dve.wait_ge(s["gpre_y"], c0["gpre_y"] + 1)
                link(dve.tensor_scalar(beta[:, :, :], bt[:, :, :], 1.0, None, ALU.add))
                link(dve.reciprocal(beta[:, :, :], beta[:, :, :]))
                link(dve.tensor_scalar(gg[:, :, :], gg[:, :, :], 0.0, None, ALU.max))
                link(dve.tensor_tensor(gg[:, :, :], gg[:, :, :], gcum[:, :, :], ALU.add))
                ea = nbeta[:, 0, :].rearrange("p (o h) -> p o h", o=1).to_broadcast([P, NT, 8])
                dve.scalar_tensor_tensor(out=gg[:, :, :], in0=gg[:, :, :], scalar=-1.0, in1=ea, op0=ALU.mult, op1=ALU.mult).then_inc(s["gpre_d"], 1)
                dve.wait_ge(s["gpre_d"], c0["gpre_d"] + 1)
                dve.wait_ge(s["gpre_mm"], c0["gpre_mm"] + 1)
                link(dve.tensor_copy(gcum[:, :, :], bank[2][:, 0:32].rearrange("p (t h) -> p t h", h=8)))
                link(dve.tensor_copy(gtot[:, :, :], bank[3][:, 0:32].rearrange("p (t h) -> p t h", h=8)))
                dve.tensor_tensor(ek[:, :, :], gtot[:, :, :], gcum[:, :, :], ALU.subtract).then_inc(s["gpre_z"], 1)
                link(dve.tensor_scalar(nbeta[:, :, :], beta[:, :, :], -1.0, None, ALU.mult))
                dve.wait_ge(s["gpre_e"], c0["gpre_e"] + 1)
                link(dve.tensor_tensor(nbg[:, :, :], nbeta[:, :, :], eg[:, :, :], ALU.mult))
                link(dve.memset(state[:, :, :], 0.0))
                dve.memset(orow[:, :, :], 0.0).then_inc(s["gpre_a"], 1)
                dve.wait_ge(s["gpre_a"], c0["gpre_a"] + 1)
                for g, pair in enumerate(scan):
                    gdn_group(s, c0, g, pair)
                t0, nt_ = act_t[0], len(act_t)
                o = orow[:, t0:, :].rearrange("p t (h j) -> p (t h) j", j=P)
                z = zrow[:, t0:, :].rearrange("p t (h j) -> p (t h) j", j=P)
                nn = 4 * nt_
                link(dve.tensor_tensor(gsq[:, 0:nn, :], o, o, ALU.mult))
                dve.tensor_reduce(ss[:, 0:nn], gsq[:, 0:nn, :], AX.X, ALU.add).then_inc(s["o_sq"], 1)
                dve.wait_ge(s["o_rs"], c0["o_rs"] + 1)
                newton(nn, 1.0 / P)
                link(dve.tensor_tensor(o, o, rstd[:, 0:nn].rearrange("p (h o) -> p h o", o=1).to_broadcast([P, nn, P]), ALU.mult))
                link(dve.tensor_tensor(o, o, per_mat(gdn_g[:, l, :], nn), ALU.mult))
                dve.tensor_tensor(o, o, z, ALU.mult).then_inc(s["o_ya"], 1)
                attention(l, s, c0)
                merge(l, s, c0)
                norm2(l, s, c0)
                route(l, s, c0)
                experts(l, s, c0)
                combine(l, s, c0)

            def gdn_group(s, c0, g, pair):
                def sig(d, ins):
                    ins.then_inc(s[f"gd{d}"], 1)

                def mine(d, name):
                    dve.wait_ge(s[f"gd{d}"], c0[f"gd{d}"] + gv(DV_SIG, g, name))

                for d, t in pair:
                    sig(d, dve.tensor_copy(gW[d][:, :, :], per_row(gg, t, 4 * d, HA)))
                for d, t in pair:
                    dve.wait_ge(s[f"gp{d}"], c0[f"gp{d}"] + gv(PE_SIG, g, "grow"))
                    link(dve.tensor_tensor(gN[d][:, :, :], heads(bank[4 * d]), per_row(gcum, t, 4 * d, HA), ALU.subtract))
                    link(dve.tensor_scalar(gE[d][:, :, :], gN[d][:, :, :], 0.0, None, ALU.max))
                    sig(d, dve.tensor_scalar(gAt[d][:, :, :], gN[d][:, :, :], 0.0, None, ALU.min))
                for d, t in pair:
                    dve.wait_ge(s[f"ga{d}"], c0[f"ga{d}"] + gv(AC_SIG, g, "exp"))
                    link(dve.tensor_tensor(gE[d][:, :, :], gE[d][:, :, :], per_mat(con("supper" if d else "slower")), ALU.mult))
                    link(dve.tensor_tensor(gE[d][:, :, :], gE[d][:, :, :], per_row(nbeta, t, 4 * d, HA), ALU.mult))
                    dve.wait_ge(s[f"gp{d}"], c0[f"gp{d}"] + gv(PE_SIG, g, "kk"))
                    sig(d, dve.tensor_tensor(gN[d][:, :, :], heads(bank[4 * d + 1]), gE[d][:, :, :], ALU.mult))
                for d, t in pair:
                    link(dve.tensor_tensor(gAt[d][:, :, :], gAt[d][:, :, :], per_mat(con("lower" if d else "upper")), ALU.mult))
                    sig(d, dve.tensor_tensor(gAt[d][:, :, :], heads(bank[4 * d + 2]), gAt[d][:, :, :], ALU.mult))
                for d, t in pair:
                    dve.wait_ge(s[f"ga{d}"], c0[f"ga{d}"] + gv(AC_SIG, g, "nt"))
                    mine(d, "n")
                    low, lowT = (gNT, gN) if d else (gN, gNT)
                    link(dve.tensor_tensor(gY[d][:, :, :], low[d][:, :, :], per_mat(con("level0")), ALU.mult))
                    link(dve.tensor_tensor(gY[d][:, :, :], gY[d][:, :, :], per_mat(ident), ALU.add))
                    link(dve.tensor_tensor(gYT[d][:, :, :], lowT[d][:, :, :], per_mat(con("level0T")), ALU.mult))
                    sig(d, dve.tensor_tensor(gYT[d][:, :, :], gYT[d][:, :, :], per_mat(ident), ALU.add))
                for k in range(1, LV):
                    for d, t in pair:
                        dve.wait_ge(s[f"gp{d}"], c0[f"gp{d}"] + gv(PE_SIG, g, f"w{k}"))
                        sig(d, dve.tensor_tensor(gW[d][:, :, :], heads(bank[4 * d]), per_mat(con(f"level{k}")), ALU.mult))
                    for d, t in pair:
                        dve.wait_ge(s[f"gp{d}"], c0[f"gp{d}"] + gv(PE_SIG, g, f"y{k}"))
                        mine(d, "lvl0" if k == 1 else f"y{k - 1}")
                        if k < LV - 1:
                            link(dve.tensor_tensor(gY[d][:, :, :], heads(bank[4 * d + 1]), gY[d][:, :, :], ALU.add))
                            sig(d, dve.tensor_tensor(gYT[d][:, :, :], heads(bank[4 * d + 2]), gYT[d][:, :, :], ALU.add))
                        else:
                            y = gY[d] if d else gYT[d]
                            sig(d, dve.tensor_tensor(y[:, :, :], heads(bank[4 * d + (1 if d else 2)]), y[:, :, :], ALU.add))
                for d, t in pair:
                    v = vrow[:, t, :].rearrange("p (h j) -> p h j", j=P)
                    dve.wait_ge(s[f"gp{d}"], c0[f"gp{d}"] + gv(PE_SIG, g, "ks"))
                    link(dve.tensor_tensor(gE[d][:, :, :], v, per_row(beta, t, 4 * d, HA), ALU.mult))
                    link(dve.tensor_tensor(gN[d][:, :, :], heads(bank[4 * d]), per_row(nbg, t, 4 * d, HA), ALU.mult))
                    sig(d, dve.tensor_tensor(gN[d][:, :, :], gN[d][:, :, :], gE[d][:, :, :], ALU.add))
                for d, t in pair:
                    dve.wait_ge(s[f"ga{d}"], c0[f"ga{d}"] + gv(AC_SIG, g, "vn"))
                    mine(d, "r")
                    sig(d, dve.tensor_tensor(gE[d][:, :, :], gNT[d][:, :, :], per_row(ek, t, 4 * d, HA), ALU.mult))
                for d, t in pair:
                    o = orow[:, t, :].rearrange("p (h j) -> p h j", j=P)
                    dve.wait_ge(s[f"gp{d}"], c0[f"gp{d}"] + gv(PE_SIG, g, "qs"))
                    link(dve.tensor_tensor(gN[d][:, :, :], heads(bank[4 * d + 1]), per_row(eg, t, 4 * d, HA), ALU.mult))
                    link(dve.tensor_tensor(gN[d][:, :, :], heads(bank[4 * d + 2]), gN[d][:, :, :], ALU.add))
                    sig(d, dve.tensor_tensor(o, o, gN[d][:, :, :], ALU.add))
                for d, t in pair:
                    st = state[:, 4 * d:4 * d + 4, :]
                    dve.wait_ge(s[f"gp{d}"], c0[f"gp{d}"] + gv(PE_SIG, g, "kv"))
                    link(dve.tensor_tensor(st, st, per_row(egt, t, 4 * d, HA), ALU.mult))
                    sig(d, dve.tensor_tensor(st, heads(bank[4 * d]), st, ALU.add))
                for d, t in pair:
                    mine(d, "state")

            def attention(l, s, c0):
                dve.wait_ge(s["o_ya"], c0["o_ya"] + 1)
                for t in (2, 3):
                    hh = HB + GB
                    x = arow[:, t, A_Q:A_V]
                    x5 = x.rearrange("p (h a b c) -> p (h a) b c", a=2, b=2, c=16)
                    tmp = rtmp[:, t - 2, :]
                    t5 = tmp.rearrange("p (h a b c) -> p (h a) b c", a=2, b=2, c=16)
                    sn = con(f"sin{t - 2}").rearrange("p (a b c) -> p a b c", a=2, b=2)
                    for h in range(hh):
                        for b in range(2):
                            last = dve.tensor_tensor(t5[:, 2 * h:2 * h + 2, b, :], x5[:, 2 * h:2 * h + 2, 1 - b, :], sn[:, :, b, :], ALU.mult)
                    link(last)
                    cs = con(f"cos{t - 2}").rearrange("p (o n) -> p o n", o=1).to_broadcast([P, hh, DH])
                    xh = x.rearrange("p (h n) -> p h n", n=DH)
                    link(dve.tensor_tensor(xh, xh, cs, ALU.mult))
                    link(dve.tensor_tensor(x, x, tmp, ALU.add))
                link(dve.tensor_copy(kswap[:, :, 0:DH], arow[:, :, A_K + DH:A_K + 2 * DH]))
                dve.tensor_copy(kswap[:, :, DH:2 * DH], arow[:, :, A_K:A_K + DH]).then_inc(s["rope"], 1)
                dve.wait_ge(s["kt_mm"], c0["kt_mm"] + 1)
                link(dve.tensor_copy(kTA, bank[0][:, :]))
                dve.tensor_copy(kTB, bank[1][:, :]).then_inc(s["kt_ev"], 1)
                for j, t in enumerate(active(l)):
                    dve.wait_ge(s["kt_mm"], c0["kt_mm"] + 2 + j)
                    dve.tensor_copy(qT[:, t, :], bank[2 + j][:, :]).then_inc(s["kt_ev"], 1)
                units = att_units(l)
                for n in range(len(units) + 1):
                    if n < len(units):
                        j, t, h, keys, masked = units[n]
                        sc = bank[n % 2]
                        dve.wait_ge(s["at_s"], c0["at_s"] + n + 1)
                        if masked is not None:
                            m = sc[:, masked * P:(masked + 1) * P]
                            link(dve.tensor_tensor(m, m, con(f"band{t - 2}"), ALU.add))
                        link(dve.reduce_max(mx[:, t, h:h + 1], sc[:, 0:keys], AX.X))
                        dve.tensor_scalar(nm[:, t, h:h + 1], mx[:, t, h:h + 1], -SCALE, nsink[:, l, h:h + 1],
                                          ALU.mult, ALU.min).then_inc(s["at_nm"], 1)
                    if n >= 1:
                        j, t, h, keys, _ = units[n - 1]
                        dve.wait_ge(s["at_tr"], c0["at_tr"] + n)
                        if n >= 3:
                            dve.wait_ge(s["at_o"], c0["at_o"] + n - 2)
                        dve.tensor_copy(probT[:, (n - 1) % 2, 0:keys], bank[2 + (n - 1) % 2][:, 0:keys]).then_inc(s["at_tev"], 1)
                        if h == HB - 1:
                            dve.wait_ge(s["at_o"], c0["at_o"] + n)
                            link(dve.tensor_tensor(den[:, t, :], den[:, t, :], esk[:, t, :], ALU.add))
                            link(dve.reciprocal(den[:, t, :], den[:, t, :]))
                            dve.tensor_tensor(yb[:, t, :].rearrange("p (h d) -> p h d", d=DH),
                                              bank[4 + j % 2][:, :].rearrange("p (h d) -> p h d", d=DH),
                                              den[:, t, :].rearrange("p (h o) -> p h o", o=1).to_broadcast([P, HB, DH]),
                                              ALU.mult).then_inc(s["at_y"], 1)

            def merge(l, s, c0):
                act_t = active(l)
                n = 0
                for dst in (yaT, ybT):
                    for t in act_t:
                        dve.wait_ge(s["mT_mm"], c0["mT_mm"] + n + 1)
                        dve.tensor_copy(dst[:, :, t * P:(t + 1) * P], bank[6 + n % 2][:, :].rearrange("p (k j) -> p k j", j=P)).then_inc(s["mT_ev"], 1)
                        n += 1
                n = 0
                for half in range(2):
                    for t in act_t:
                        u = n % 2
                        bk = bank[4 * u:4 * u + 4]
                        dve.wait_ge(s["mg_a"], c0["mg_a"] + n + 1)
                        for x in (ga, gb):
                            link(dve.tensor_scalar(x[:, u, :], x[:, u, :], 1.0, None, ALU.add))
                            link(dve.reciprocal(x[:, u, :], x[:, u, :]))
                        link(dve.tensor_tensor(pa[:, u, :], bk[2][:, :], ga[:, u, :], ALU.mult))
                        link(dve.tensor_tensor(pb[:, u, :], bk[3][:, :], gb[:, u, :], ALU.mult))
                        dve.tensor_tensor(mrow[:, t, half * 512:(half + 1) * 512], pa[:, u, :], pb[:, u, :], ALU.add).then_inc(s["mg_d"], 1)
                        n += 1
                for j, t in enumerate(act_t):
                    for q in range(2):
                        dve.wait_ge(s["m2_mm"], c0["m2_mm"] + 2 * j + q + 1)
                        dve.tensor_copy(HT[:, 4 * q:4 * q + 4, t * P:(t + 1) * P],
                                        bank[2 * (j % 2) + q][:, :].rearrange("p (k j) -> p k j", j=P)).then_inc(s["m2_ev"], 1)
                dve.wait_ge(s["g1load"], c0["g1load"] + 32)
                n = 0
                for half in range(2):
                    cs = slice(half * 512, (half + 1) * 512)
                    for t in act_t:
                        dve.wait_ge(s["y_mm"], c0["y_mm"] + n + 1)
                        link(dve.tensor_tensor(pa[:, n % 2, :], bank[4 + n % 2][:, :], g1bc[:, stream(t), cs], ALU.mult))
                        dve.tensor_tensor(X[:, t, cs], X[:, t, cs], pa[:, n % 2, :], ALU.add).then_inc(s["y_ev"], 1)
                        n += 1

            def norm2(l, s, c0):
                act_t = active(l)
                nn = len(act_t)
                dve.wait_ge(s["n2rs0"], c0["n2rs0"] + 1)
                newton(nn, 1.0 / D)
                dve.wait_ge(s["bcload"], c0["bcload"] + 80)
                for j in range(nn + 1):
                    if j < nn:
                        t = act_t[j]
                        if j >= 2:
                            dve.wait_ge(s[f"h2st{j % 2}"], c0[f"h2st{j % 2}"] + 16 * (j // 2))
                            dve.wait_ge(s["r_tr"], c0["r_tr"] + j - 1)
                        link(dve.scalar_tensor_tensor(out=h2[:, j % 2, :], in0=X[:, t, :], scalar=rstd[:, j:j + 1], in1=g2n[:, stream(t), :],
                                                      op0=ALU.mult, op1=ALU.mult))
                        dve.tensor_tensor(h2[:, j % 2, :], h2[:, j % 2, :], sh2bc[:, stream(t), :], ALU.add).then_inc(s["h2row"], 1)
                    if j >= 1:
                        q = j - 1
                        dve.wait_ge(s["r_tr"], c0["r_tr"] + q + 1)
                        if q >= 2:
                            dve.wait_ge(s["r_mm"], c0["r_mm"] + q - 1)
                        link(dve.tensor_copy(h2T[:, q % 2, 0:512], bank[0][:, :]))
                        dve.tensor_copy(h2T[:, q % 2, 512:1024], bank[1][:, :]).then_inc(s["r_tev"], 1)

            def route(l, s, c0):
                act_t = active(l)
                nn = len(act_t)
                t0 = act_t[0]
                A = lambda x: x[:, 0:nn, :]
                B1 = lambda x, n: x[:, 0:nn].rearrange("p (t o) -> p t o", o=1).to_broadcast([P, nn, n])
                row = lambda x, n: x.rearrange("p (o e) -> p o e", o=1).to_broadcast([P, nn, n])
                score, sel, msel, oh1, oh2, hot, key, rank = (rt[i] for i in (1, 2, 3, 4, 6, 5, 7, 8))
                dve.wait_ge(s["r_a"], c0["r_a"] + 1)
                link(dve.tensor_scalar(A(score), A(rt[0]), 1.0, None, ALU.add))
                link(dve.reciprocal(A(score), A(score)))
                link(dve.tensor_tensor(A(sel), A(score), row(rbias, NE), ALU.add))
                s4 = A(sel).rearrange("p t (g e) -> p t g e", e=4)
                pr = rp[:, 0:nn, :, :]
                for t in range(nn):
                    link(dve.tensor_tensor(pr[:, t, :, 0:3], s4[:, t, :, 0:3], s4[:, t, :, 1:4], ALU.add))
                    link(dve.tensor_tensor(pr[:, t, :, 3:5], s4[:, t, :, 0:2], s4[:, t, :, 2:4], ALU.add))
                    link(dve.tensor_tensor(pr[:, t, :, 5:6], s4[:, t, :, 0:1], s4[:, t, :, 3:4], ALU.add))
                for t in range(nn):
                    link(dve.reduce_max(rg[0][:, t, :], pr[:, t, :, :], AX.X))
                link(dve.reduce_max(r1[0][:, 0:nn], A(rg[0]), AX.X))
                link(dve.tensor_tensor(A(rg[1]), A(rg[0]), B1(r1[0], NG), ALU.is_equal))
                link(dve.tensor_tensor(A(rg[1]), A(rg[1]), row(con("grouprank"), NG), ALU.mult))
                link(dve.reduce_max(r1[0][:, 0:nn], A(rg[1]), AX.X))
                link(dve.tensor_tensor(A(rg[1]), A(rg[1]), B1(r1[0], NG), ALU.is_equal))
                for t in range(nn):
                    link(dve.tensor_copy(key[:, t, :].rearrange("p (g e) -> p g e", e=4),
                                         rg[1][:, t, :].rearrange("p (g o) -> p g o", o=1).to_broadcast([P, NG, 4])))
                link(dve.tensor_tensor(A(msel), A(sel), A(key), ALU.mult))
                link(dve.tensor_scalar(A(key), A(key), 1e30, -1e30, ALU.mult, ALU.add))
                link(dve.tensor_tensor(A(msel), A(msel), A(key), ALU.add))
                for oh in (oh1, oh2):
                    link(dve.reduce_max(r1[0][:, 0:nn], A(msel), AX.X))
                    link(dve.tensor_tensor(A(key), A(msel), B1(r1[0], NE), ALU.is_equal))
                    link(dve.tensor_tensor(A(key), A(key), row(con("expertrank"), NE), ALU.mult))
                    link(dve.reduce_max(r1[0][:, 0:nn], A(key), AX.X))
                    link(dve.tensor_tensor(A(oh), A(key), B1(r1[0], NE), ALU.is_equal))
                    link(dve.scalar_tensor_tensor(out=A(msel), in0=A(oh), scalar=-1e31, in1=A(msel), op0=ALU.mult, op1=ALU.add))
                dve.tensor_tensor(A(hot), A(oh1), A(oh2), ALU.add).then_inc(s["r_hot"], 1)
                for j, oh in enumerate((oh1, oh2)):
                    link(dve.tensor_tensor(A(key), A(oh), A(score), ALU.mult))
                    link(dve.reduce_sum(r1[1 + j][:, 0:nn], A(key), AX.X))
                link(dve.tensor_tensor(r1[3][:, 0:nn], r1[1][:, 0:nn], r1[2][:, 0:nn], ALU.add))
                link(dve.reciprocal(r1[3][:, 0:nn], r1[3][:, 0:nn]))
                for j in range(2):
                    link(dve.tensor_tensor(wkeep[:, j, 0:nn], r1[1 + j][:, 0:nn], r1[3][:, 0:nn], ALU.mult))
                dve.wait_ge(s["r_rank"], c0["r_rank"] + 1)
                cnt, nb, inc, start, tmp, one = re
                link(dve.tensor_copy(cnt, bank[4][:, 0:NE]))
                link(dve.tensor_scalar(nb, cnt, 0.0, None, ALU.is_gt))
                for k in range(1, nn):
                    link(dve.tensor_scalar(tmp, cnt, float(P * k), None, ALU.is_gt))
                    link(dve.tensor_tensor(nb, nb, tmp, ALU.add))
                link(dve.memset(one, 1.0))
                link(dve.tensor_tensor_scan(inc, one, nb, 0.0, ALU.mult, ALU.add))
                link(dve.tensor_tensor(start, inc, nb, ALU.subtract))
                link(dve.tensor_scalar(tmp, start, float(P), None, ALU.mult))
                link(dve.tensor_tensor(A(rank), bank[3][:, 0:nn * NE].rearrange("p (t e) -> p t e", e=NE), row(tmp, NE), ALU.add))
                for j, oh in enumerate((oh1, oh2)):
                    link(dve.tensor_tensor(A(key), A(oh), A(rank), ALU.mult))
                    link(dve.reduce_sum(r1[4 + j][:, 0:nn], A(key), AX.X))
                    link(dve.tensor_copy(pos_u[:, j, t0:NT], r1[4 + j][:, 0:nn]))
                    link(dve.tensor_copy(pos_i[:, 0, j, 0:nn], r1[4 + j][:, 0:nn]))
                    link(dve.tensor_scalar(pos_i[:, 1, j, 0:nn], pos_i[:, 0, j, 0:nn], P - 1, None, ALU.bitwise_and))
                    link(dve.tensor_scalar(pos_i[:, 2, j, 0:nn], pos_i[:, 0, j, 0:nn], 7, None, ALU.logical_shift_right))
                    link(dve.tensor_copy(r1[6 + j][:, 0:nn], pos_i[:, 1, j, 0:nn]))
                    link(dve.tensor_copy(r1[8 + j][:, 0:nn], pos_i[:, 2, j, 0:nn]))
                for j in range(2):
                    for t in range(nn):
                        q = 2 * t + j
                        link(dve.tensor_scalar(hot_r[:, q, :], con("iota"), r1[6 + j][:, t:t + 1], None, ALU.is_equal))
                        last = dve.tensor_scalar(hot_b[:, q, :], con("iota")[:, 0:NBLK], r1[8 + j][:, t:t + 1],
                                                 con("token")[:, t0 + t:t0 + t + 1], ALU.is_equal, ALU.mult)
                        if q < 2 * nn - 1:
                            link(last)
                last.then_inc(s["r_sort"], 1)
                dve.wait_ge(s["r_sort"], c0["r_sort"] + 1)
                link(dve.tensor_tensor(cmpb[:, :, :], con("iota")[:, 0:NBLK].rearrange("p (b o) -> p b o", o=1).to_broadcast([P, NBLK, NE]),
                                       start.rearrange("p (o e) -> p o e", o=1).to_broadcast([P, NBLK, NE]), ALU.is_ge))
                link(dve.reduce_sum(blk_e[:, 0:NBLK], cmpb[:, :, :], AX.X))
                link(dve.tensor_scalar(blk_e[:, 0:NBLK], blk_e[:, 0:NBLK], -1.0, None, ALU.add))
                link(dve.tensor_copy(blk_e[:, NBLK:NBLK + 1], inc[:, NE - 1:NE]))
                link(dve.tensor_copy(meta[:, :], blk_e))
                dve.wait_ge(s["r_inv"], c0["r_inv"] + 1)
                dve.tensor_copy(slot_tok[:, :], bank[5][:, 0:NBLK]).then_inc(s["routed"], 1)

            def experts(l, s, c0):
                nblk = dve.value_load(meta[0:1, NBLK:NBLK + 1], min_val=1, max_val=NBLK)
                dve.sem_inc(s["ed_ev0"], 1)
                with dve.Fori(0, NBLK // 2) as i:
                    for u in range(2):
                        b = i * 2 + u
                        with dve.If(b < nblk):
                            dve.wait_ge(s["xg_mm"], b + 3)
                            dve.tensor_copy(xT[:, u, 0:512], bank[0][:, :]).then_inc(s["xg_ev0"], 1)
                            dve.wait_ge(s["eu_mm"], b + 3)
                            dve.wait_ge(s["e_silu"], b + 1)
                            dve.tensor_tensor(he[:, u, :], bank[3][:, :], eg_s[:, u, :], ALU.mult).then_inc(s["e_he"], 1)
                            dve.wait_ge(s[f"st{u}"], (i + 1) * 16)
                            dve.wait_ge(s["ed_mm"], b + 3)
                            dve.tensor_copy(yrow[:, u, 0:512], bank[5][:, :]).then_inc(s["ed_ev0"], 1)

            def combine(l, s, c0):
                act_t = active(l)
                dve.wait_ge(s["g2load"], c0["g2load"] + 32)
                for j, t in enumerate(act_t):
                    dve.wait_ge(s[f"ygl{j % 2}"], c0[f"ygl{j % 2}"] + 32 * (j // 2 + 1))
                    y1, y2 = yg[:, 2 * (j % 2), :], yg[:, 2 * (j % 2) + 1, :]
                    link(dve.tensor_scalar(y1, y1, wkeep[:, 0, j:j + 1], None, ALU.mult))
                    link(dve.scalar_tensor_tensor(out=y1, in0=y2, scalar=wkeep[:, 1, j:j + 1], in1=y1, op0=ALU.mult, op1=ALU.add))
                    link(dve.tensor_tensor(y1, y1, g2bc[:, stream(t), :], ALU.mult))
                    dve.tensor_tensor(X[:, t, :], X[:, t, :], y1, ALU.add).then_inc(s["comb"], 1)
                if l == DEPTH - 1:
                    dve.wait_ge(once["f_rs"], 1)
                    newton(2, 1.0 / D)
                    dve.wait_ge(fin_load, 16)
                    for j, t in enumerate(act_t):
                        dve.scalar_tensor_tensor(out=X[:, t, :], in0=X[:, t, :], scalar=rstd[:, j:j + 1], in1=fg,
                                                 op0=ALU.mult, op1=ALU.mult).then_inc(once["f_out"], 1)

            for l in range(DEPTH):
                layer(l)


_INS = ["x", "c", "ctx", "c_ctx", "w_mod", "b_mod", "norm1_g", "norm2_g", "w_in", "conv_w", "a_log", "dt_bias",
        "gdn_norm_g", "sink", "w_oa", "w_ob", "w_o", "w_router", "router_bias", "w_gate", "w_up", "w_down", "final_g"]


def kernel(**inputs):
    import concourse.bacc as _bacc
    from concourse.bass_utils import run_bass_kernel_spmd as _run

    nc = _bacc.Bacc("TRN2", target_bir_lowering=False, num_devices=1)
    arrays, args = {}, {}
    for name in _INS:
        v = np.ascontiguousarray(inputs[name])
        arrays[f"in_{name}"] = v
        args[name] = nc.dram_tensor(f"in_{name}", v.shape, mybir.dt.from_np(v.dtype), kind="ExternalInput").ap()
    table = np.ascontiguousarray(constants()[0])
    arrays["in_table"] = table
    args["table"] = nc.dram_tensor("in_table", table.shape, F32, kind="ExternalInput").ap()
    out = nc.dram_tensor("out_0", (1, SEQ, D), F32, kind="ExternalOutput").ap()
    build(nc, args, out)
    r = _run(nc, [arrays], core_ids=[0])
    return r.results[0]["out_0"]
```

```python
from contextlib import ExitStack

import concourse.bass as bass
import numpy as np
from concourse import mybir

F32 = mybir.dt.float32
I32 = mybir.dt.int32
U32 = mybir.dt.uint32
ALU = mybir.AluOpType
ACT = mybir.ActivationFunctionType
AX = mybir.AxisListType

P = 128
D = 1024
KD = D // P
SEQ = 256
NT = 4
DEPTH = 2
EPS = 1e-6
HA = 4
HB, GB, DH = 8, 2, 64
NE, NG = 16, 4
FE = 512
KF = FE // P
CONV = 5
CHT = 12
GRID_W = 64
C_Z, C_BA, C_GA, C_GB, C_END = 1536, 2048, 2832, 3856, 4880
AROW = C_GA - C_BA
A_Q, A_K, A_V = 16, 528, 656
SLOTS = 4
LV = 7
ROWS = (4, 5, 3)
MOD_EARLY = 8
MOD_ORDER = (tuple(range(12)), tuple(range(12 - MOD_EARLY, 12)) + tuple(range(12 - MOD_EARLY)))
NBLK = 24
SCALE = DH ** -0.5


def constants():
    i = np.arange(P)[:, None]
    j = np.arange(P)[None, :]
    parts = {"ident": i == j, "ones": np.ones((P, P)), "upper": i <= j, "lower": i >= j,
             "supper": i < j, "slower": i > j}
    for k in range(LV):
        below = (i >> (k + 1) == j >> (k + 1)) & ((i >> k) & 1 == 1) & ((j >> k) & 1 == 0)
        parts[f"level{k}"] = below | (i == j)
    parts["level0T"] = parts["level0"].T
    nf = DH // 4
    inv = (np.float32(10000.0) ** (-np.arange(nf, dtype=np.float32) / np.float32(nf))).astype(np.float32)
    pos = np.arange(SEQ)
    ang = [(q.astype(np.float32)[:, None] * inv[None, :]).astype(np.float32) for q in (pos // GRID_W, pos % GRID_W)]
    cos = np.concatenate([np.cos(ang[0]), np.cos(ang[0]), np.cos(ang[1]), np.cos(ang[1])], 1)
    sin = np.concatenate([-np.sin(ang[0]), np.sin(ang[0]), -np.sin(ang[1]), np.sin(ang[1])], 1)
    for n in range(2):
        parts[f"cos{n}"] = cos[n * P:(n + 1) * P]
        parts[f"sin{n}"] = sin[n * P:(n + 1) * P]
    parts["band0"] = np.where(j <= i, 0.0, -1e30)
    parts["band1"] = np.where(i <= j, 0.0, -1e30)
    parts["iota"] = np.broadcast_to(j, (P, P))
    parts["token"] = i + P * np.arange(NT)[None, :]
    parts["grouprank"] = np.broadcast_to(8 - np.arange(NG), (P, NG))
    parts["expertrank"] = np.broadcast_to(32 - np.arange(NE), (P, NE))
    parts["eps"] = np.full((P, 1), EPS)
    at, off = {}, 0
    for k, v in parts.items():
        at[k] = (off, v.shape[1])
        off += v.shape[1]
    return np.concatenate([np.asarray(v, np.float32) for v in parts.values()], 1), at


def build(nc, a, out):
    table, at = constants()
    ctx = ExitStack()
    with ctx:
        def sb(name, shape, dt=F32):
            return ctx.enter_context(nc.sbuf_tensor(name, shape, dt))

        def scratch(name, shape, dt=F32):
            return nc.dram_tensor(name, shape, dt).ap()

        mod_dram = [scratch(f"mod_rows{l}", (2, 6 * D)) for l in range(DEPTH)]
        h2_dram = scratch("h2_rows", (NT * P, D))
        y_dram = scratch("expert_rows", (NBLK * P, D))

        CON = sb("CON", [P, table.shape[1]])
        X = sb("X", [P, NT, D])
        HT = sb("HT", [P, KD, NT * P])
        RING = sb("RING", [P, 6, KD * 512])
        WORK = sb("WORK", [P, 16448])
        small = sb("small", [P, 1100])
        meta = sb("meta", [P, NBLK + 1], I32)
        slot_tok = sb("slot_tok", [P, NBLK + 1], U32)
        cur_tok = sb("cur_tok", [P, 2], U32)
        pos_u = sb("pos_u", [P, 2, NT], U32)
        pos_i = sb("pos_i", [P, 3, 2, NT], I32)
        bank = [ctx.enter_context(nc.psum_tensor(f"bank{i}", [P, 512], F32)) for i in range(8)]

        def con(name):
            o, n = at[name]
            return CON[:, o:o + n]

        ident = con("ident")

        def carve(base, start):
            pos = [start]

            def take(*shape):
                n = int(np.prod(shape))
                v = base[:, pos[0]:pos[0] + n]
                pos[0] += n
                assert pos[0] <= base.shape[1]
                if len(shape) == 2:
                    v = v.rearrange("p (a b) -> p a b", b=shape[1])
                elif len(shape) == 3:
                    v = v.rearrange("p (a b c) -> p a b c", b=shape[1], c=shape[2])
                return v
            return take

        tk = carve(small, 0)
        modT = tk(KD, 4)
        sT = tk(KD, 2)
        crow_T = tk(KD, 2)
        convT = tk(DEPTH, CONV * CHT)
        alog, dtb, nsink, rbias = tk(DEPTH, 8), tk(DEPTH, 8), tk(DEPTH, HB), tk(NE)
        gdn_g = tk(DEPTH, P)
        ss, rstd, st1, st2 = tk(16), tk(16), tk(16), tk(16)
        beta, gg, gcum, gtot = tk(NT, 8), tk(NT, 8), tk(NT, 8), tk(NT, 8)
        eg, egt, ek, nbg, nbeta, bt = tk(NT, 8), tk(NT, 8), tk(NT, 8), tk(NT, 8), tk(NT, 8), tk(NT, 8)
        mx, nm, den, esk = tk(NT, HB), tk(NT, HB), tk(NT, HB), tk(NT, HB)
        wkeep = tk(2, NT)

        slot45 = RING[:, SLOTS:6, :].rearrange("p a b -> p (a b)")

        tk = carve(WORK, 0)
        modrow0 = tk(6 * D)
        gnorm0 = tk(2, D)
        crow, cwrow = tk(P), tk(DEPTH, P)
        tk = carve(WORK, 9216)
        gnorm1, _, modrow1 = tk(1, D), tk(64), tk(6 * D)
        modrow, gnorm = (modrow0, modrow1), ((gnorm0[:, 0, :], gnorm0[:, 1, :]), (gnorm1[:, 0, :], gnorm1[:, 0, :]))
        tk = carve(WORK, 10000)
        nsq0, xn0 = tk(D), tk(NT, D)
        nsq, xn = (nsq0, WORK[:, 8192:9216]), (xn0, WORK[:, 0:NT * D].rearrange("p (t n) -> p t n", n=D))
        tk = carve(WORK, 0)
        QK = tk(8, NT * P)
        krow, vrow = tk(NT, HA * P), tk(NT, HA * P)
        zrow = tk(NT, HA * P)
        arow = tk(NT, AROW)
        state = tk(2 * HA, P)
        orow = tk(NT, HA * P)
        tk = carve(slot45, 0)
        rtmp = slot45[:, 5200:5200 + 2 * (HB + GB) * DH].rearrange("p (t n) -> p t n", t=2)
        kswap = slot45[:, 7680:8192].rearrange("p (t n) -> p t n", t=NT)
        zero_tile = slot45[:, 7168:7680]
        cpad, cy, vT, sq = tk(2, 2 * (SEQ + 4)), tk(2, 512), tk(4, 512), tk(2, 512)
        tk = carve(slot45, 0)
        gN, gNT, gY, gYT, gW, gE, gAt = ([tk(HA, P) for _ in range(2)] for _ in range(7))
        tk = carve(slot45, 0)
        qT, kTA, kTB = tk(NT, 4 * P), tk(NT * P), tk(NT * P)
        prob, probT = tk(2, 512), tk(2, 512)
        gsq = tk(NT * HA, P)
        yb = QK[:, 0:4, :]
        yaT, ybT = QK[:, 4:8, :], krow
        mrow = WORK[:, 6144:6144 + NT * D].rearrange("p (t n) -> p t n", n=D)
        tk = carve(slot45, 0)
        ga, gb = tk(NT, 512), tk(NT, 512)
        g1bc = tk(2, D)
        pa, pb = tk(2, 512), tk(2, 512)
        tk = carve(WORK, 0)
        h2 = slot45[:, 0:NT * D].rearrange("p (t n) -> p t n", n=D)
        tk(2, D)
        h2sq, h2T = tk(D), tk(2, D)
        g2n, sh2bc = tk(2, D), tk(2, D)
        wr = tk(KD, NE)
        rt = [tk(NT, NE) for _ in range(14)]
        rg = [tk(NT, NG) for _ in range(5)]
        rp = tk(NT, NG, 6)
        r1 = [tk(NT) for _ in range(12)]
        wts = tk(2, NT)
        hot_r, hot_b = tk(2 * NT, P), tk(2 * NT, NBLK)
        re = [tk(NE) for _ in range(6)]
        cmpb, blk_e = tk(NBLK, NE), tk(NBLK + 1)
        tk = carve(WORK, 0)
        xg, xT, eg_s, he, heT, yrow = tk(2, D), tk(2, D), tk(2, FE), tk(2, FE), tk(2, FE), tk(2, D)
        tk = carve(WORK, 0)
        yg = tk(2 * NT, D)
        tk = carve(slot45, 0)
        g2bc, fg, fsq = tk(2, D), tk(D), tk(D)

        PE_SIG = ["grow", "kk", "nt"] + [f"{x}{k}" for k in range(1, LV - 1) for x in "wyt"] + ["w6", "f6", "ks", "xr", "qs", "kv"]
        DV_SIG = ["gb", "clamp", "n", "attn", "lvl0"] + [f"{x}{k}" for k in range(1, LV - 1) for x in "wt"] + ["w6", "f6", "r", "vs", "o", "state"]
        AC_SIG = ["exp", "nt"] + [f"y{k}" for k in range(1, LV - 1)] + ["vn"]

        per_layer = {
            "b_load": 96, "modmm": 12, "modev": 12, "modfold": 2, "modT_mm": 1, "modT_ev": 1, "modstore": 16, "bcload": 80,
            "rs0": 1, "xn": NT, "xt_mm": NT, "xt_ev": NT, "xt_ea": NT, "pj_mm": CHT, "pj_pad": CHT, "pj_conv": CHT, "pj_silu": CHT,
            "l2sq": 8, "l2mm": 8, "l2ln": 8, "l2out": 8, "tr_mm": 8, "tr_ev": 8, "row_mm": 3 * NT, "row_ev": 3 * NT,
            "gpre_a": 1, "gpre_d": 1, "gpre_mm": 1, "gpre_x": 1, "gpre_y": 1, "gpre_z": 1, "gpre_e": 1,
            "gp0": 4 * len(PE_SIG), "gp1": 4 * len(PE_SIG), "gd0": 4 * len(DV_SIG), "gd1": 4 * len(DV_SIG),
            "ga0": 4 * len(AC_SIG), "ga1": 4 * len(AC_SIG), "o_sq": 1, "o_rs": 1, "o_ya": NT,
            "kt_mm": 1 + NT, "kt_ev": 1 + NT, "at_s": NT * HB, "at_nm": NT * HB, "at_p": NT * HB, "at_tr": NT * HB,
            "at_tev": NT * HB, "at_o": NT * HB, "at_y": NT, "mT_mm": 2 * NT, "mT_ev": 2 * NT, "mg_mm": 8 * NT,
            "mg_a": 4 * NT, "mg_d": 4 * NT, "m2_mm": 2 * NT, "m2_ev": 2 * NT, "y_mm": 2 * NT, "y_ev": 2 * NT,
            "g1load": 32, "n2rs0": 1, "h2row": NT, "h2st0": 32, "h2st1": 32, "r_tr": NT, "r_tev": NT, "r_mm": NT, "r_a": 1,
            "r_hot": 1, "r_rank": 1, "r_sort": 1, "blocks": 1, "r_inv": 1, "routed": 1, "g2load": 32, "comb": NT,
            "ygl0": 32, "ygl1": 32, "ygl2": 32, "ygl3": 32,
        }
        shared = {n: ctx.enter_context(nc.semaphore(n)) for n in per_layer}
        before = [{n: 0 for n in per_layer}, dict(per_layer)]
        looped = """xg_mm0 xg_mm1 xg_ev0 xg_ev1 eg_mm eu_mm e_silu e_he ht_mm ht_ev ed_mm ed_ev0 ed_ev1 xgl0 xgl1 wl0 wl1 wl2 wl3 wl4 wl5 idx st0 st1""".split()
        S = [{**shared, **{n: ctx.enter_context(nc.semaphore(f"{n}_{l}")) for n in looped}} for l in range(DEPTH)]
        once = {n: ctx.enter_context(nc.semaphore(n)) for n in "c_T ct_mm c_silu params f_rs f_out".split()}
        ring_loaded = [ctx.enter_context(nc.semaphore(f"ring_loaded{s}")) for s in range(SLOTS)]
        x_loaded = ctx.enter_context(nc.semaphore("x_loaded"))
        con_loaded = ctx.enter_context(nc.semaphore("con_loaded"))
        small_loaded = ctx.enter_context(nc.semaphore("small_loaded"))
        zeroed = ctx.enter_context(nc.semaphore("zeroed"))
        fin_load = ctx.enter_context(nc.semaphore("fin_load"))
        stored = ctx.enter_context(nc.semaphore("stored"))
        dve_link = ctx.enter_context(nc.semaphore("dve_link"))
        act_link = ctx.enter_context(nc.semaphore("act_link"))
        y_zeroed = ctx.enter_context(nc.semaphore("y_zeroed"))
        pool_passed = ctx.enter_context(nc.semaphore("pool_passed"))
        pool_link = ctx.enter_context(nc.semaphore("pool_link"))

        def chunks(l):
            w_in = a["w_in"][l].rearrange("(k p) n -> p k n", p=P)
            w_mod = a["w_mod"][l].rearrange("(k p) n -> p k n", p=P)
            w_o = a["w_o"][l].rearrange("(k p) n -> p k n", p=P)
            oa = a["w_oa"][l].rearrange("(k p) n -> p k n", p=P)
            ob = a["w_ob"][l].rearrange("(k p) n -> p k n", p=P)
            for c in MOD_ORDER[l]:
                yield ("mod", c), [(0, 512, w_mod[:, :, 512 * c:512 * c + 512])]
            for c in (0, 1, 2, *ROWS):
                end = min(512 * c + 512, C_GA)
                yield ("in", c), [(0, end - 512 * c, w_in[:, :, 512 * c:end])]
            for n in range(2):
                yield ("m0", n), [(0, 512, w_in[:, :, C_GA + 512 * n:C_GA + 512 * n + 512])]
                yield ("m1", n), [(0, 512, w_in[:, :, C_GB + 512 * n:C_GB + 512 * n + 512])]
                yield ("m2", n), [("lo", 512, oa[:, :, 512 * n:512 * n + 512]), ("hi", 512, ob[:, :, 512 * n:512 * n + 512])]
            for n in range(2):
                yield ("o", n), [(0, 512, w_o[:, :, 512 * n:512 * n + 512])]

        plan = [(l, key, parts) for l in range(DEPTH) for key, parts in chunks(l)]
        where = {(l, key): n for n, (l, key, _) in enumerate(plan)}
        fills = {}
        count = [0] * SLOTS
        for n, (l, key, parts) in enumerate(plan):
            count[n % SLOTS] += 16 * len(parts)
            fills[n] = count[n % SLOTS]
        first_of = [where[(l, ("mod", MOD_ORDER[l][0]))] for l in range(DEPTH)] + [len(plan)]
        after_experts = first_of[1] + MOD_EARLY

        def ring(l, key):
            n = where[(l, key)]
            return RING[:, n % SLOTS, :].rearrange("p (k n) -> p k n", n=512)

        def ring_wait(pe, l, key):
            n = where[(l, key)]
            pe.wait_ge(ring_loaded[n % SLOTS], fills[n])

        def used(n):
            l, (kind, c), _ = plan[n]
            nact = len(active(l))
            if kind == "mod":
                name, v = "modmm", MOD_ORDER[l].index(c) + 1
            elif kind == "in" and c < 3:
                name, v = "pj_mm", 4 * (c + 1)
            elif kind == "in":
                name, v = "row_mm", sum(1 for q in ROWS[:ROWS.index(c) + 1] for _ in row_parts(l, q))
            elif kind == "o":
                name, v = "y_mm", nact * (c + 1)
            else:
                name, v = "mg_mm", nact * (4 * c + {"m0": 1, "m1": 2, "m2": 4}[kind])
            return S[l][name], before[l][name] + v

        def active(l):
            return [0, 1, 2, 3] if l < DEPTH - 1 else [2, 3]

        def stream(t):
            return t // 2

        def bc(ap, *shape):
            return ap.to_broadcast([P, *shape])

        def per_row(v, t, c0, n):
            return v[:, t, c0:c0 + n].rearrange("p (h o) -> p h o", o=1).to_broadcast([P, n, P])

        def per_mat(m, n=HA):
            return m.rearrange("p (o j) -> p o j", o=1).to_broadcast([P, n, P])

        scan = [((0, 0), (1, 1)), ((0, 1), (1, 0)), ((0, 2), (1, 3)), ((0, 3), (1, 2))]
        def gv(sigs, g, name):
            return g * len(sigs) + sigs.index(name) + 1

        def row_parts(l, c):
            for t in range(NT):
                full = t in active(l)
                if c == 3:
                    if full:
                        yield t, (0, 512, 0)
                elif c == 4:
                    yield t, (0, 512 if full else 16, 0)
                else:
                    yield t, (0, 272, 512) if full else (16, 256, 528)

        def row_groups(l):
            return [(c, t, place) for c in ROWS for t, place in row_parts(l, c)]

        L2_ORDER = (4, 5, 6, 7, 0, 1, 2, 3)
        TURNS = (("v", 0), ("v", 1), ("v", 2), ("k", 0), ("v", 3), ("k", 1), ("k", 2), ("k", 3))

        def turns_at(r):
            return [x for x in (("v", r), ("k", r - 2)) if x in TURNS]

        def merge_evac(l, n):
            nact = len(active(l))
            half, step, j = n // (4 * nact), n // nact % 4, n % nact
            return ("mg_a" if step < 2 else "mg_d"), half * 2 * nact + (step % 2) * nact + j + 1

        def att_units(l):
            return [(j, t, h, 4 * P if t >= 2 else 2 * P, (5 - t) if t >= 2 else None)
                    for j, t in enumerate(active(l)) for h in range(HB)]

        def mod_bank(l, n):
            if l == 0:
                return bank[4 + n % 4][0:2, :]
            return bank[7 if n % 2 else 4 if n >= MOD_EARLY else 6][0:2, :]

        def heads(bk):
            return bk[:, :].rearrange("p (h j) -> p h j", j=P)

        block = ctx.enter_context(nc.Block())

        @block.sync
        def _(sp):
            sp.dma_start(CON[:, :], a["table"]).then_inc(con_loaded, 16)
            sp.dma_start(crow[0:8, :], a["c_ctx"].rearrange("(k p) -> k p", p=P)).then_inc(small_loaded, 16)
            sp.dma_start(crow[8:16, :], a["c"].rearrange("o (k p) -> (o k) p", p=P)).then_inc(small_loaded, 16)
            for l in range(DEPTH):
                sp.dma_start(cwrow[0:CONV * CHT, l, :], a["conv_w"][l].rearrange("j (t p) -> (j t) p", p=P)).then_inc(small_loaded, 16)

            def load_chunk(n):
                l, key, parts = plan[n]
                if n - SLOTS >= (after_experts if n >= after_experts else 0):
                    sp.wait_ge(*used(n - SLOTS))
                for k0, width, src in parts:
                    dst = RING[:, n % SLOTS, :].rearrange("p (k n) -> p k n", n=512)
                    dst = dst[:, 4:8, :] if k0 == "hi" else dst[:, 0:4, :] if k0 == "lo" else dst[:, :, 0:width]
                    sp.dma_start(dst, src).then_inc(ring_loaded[n % SLOTS], 16)

            def layer(l):
                s, c0 = S[l], before[l]
                n0 = first_of[l]
                if l == 0:
                    for r in range(2):
                        sp.dma_start(modrow[0][r:r + 1, :], a["b_mod"][0:1, :]).then_inc(s["b_load"], 16)
                        for j, g in enumerate(("norm1_g", "norm2_g")):
                            sp.dma_start(gnorm[0][j][r:r + 1, :], a[g][0:1, :]).then_inc(s["b_load"], 16)
                    for n in range(12):
                        load_chunk(n)
                        if n == 3:
                            sp.dma_start(X[:, 0:2, :], a["ctx"].rearrange("o (t p) d -> p (o t) d", p=P)).then_inc(x_loaded, 16)
                            sp.dma_start(X[:, 2:4, :], a["x"].rearrange("o (t p) d -> p (o t) d", p=P)).then_inc(x_loaded, 16)
                else:
                    for r in range(2):
                        early = 512 * (12 - MOD_EARLY)
                        sp.dma_start(modrow[1][r:r + 1, 0:early], a["b_mod"][1:2, 0:early]).then_inc(s["b_load"], 16)
                        sp.dma_start(gnorm[1][1][r:r + 1, :], a["norm2_g"][1:2, :]).then_inc(s["b_load"], 16)
                    for n in range(after_experts, n0 + 12):
                        if n > after_experts:
                            sp.wait_ge(S[0][f"ygl{n - after_experts}"], 32)
                        load_chunk(n)
                    sp.wait_ge(s["modfold"], c0["modfold"] + 1)
                    for r in range(2):
                        sp.dma_start(gnorm[1][0][r:r + 1, :], a["norm1_g"][1:2, :]).then_inc(s["b_load"], 16)
                for n in range(n0 + 12, first_of[l + 1] + (2 if l == 0 else 0)):
                    load_chunk(n)
                    if n == n0 + 19:
                        sp.wait_ge(s["modstore"], c0["modstore"] + 16)
                        sp.wait_ge(s["at_y"], c0["at_y"] + len(active(l)))
                        for st in range(2):
                            sp.dma_start(g1bc[:, st, :], mod_dram[l][st:st + 1, 2 * D:3 * D].to_broadcast([P, D])).then_inc(s["g1load"], 16)
                sp.wait_ge(s["m2_mm"], c0["m2_mm"] + len(active(l)) * 2)
                for st in range(2):
                    sp.dma_start(sh2bc[:, st, :], mod_dram[l][st:st + 1, 3 * D:4 * D].to_broadcast([P, D])).then_inc(s["bcload"], 16)
                    sp.dma_start(g2n[:, st, :], mod_dram[l][st:st + 1, 4 * D:5 * D].to_broadcast([P, D])).then_inc(s["bcload"], 16)
                sp.dma_start(wr, a["w_router"].rearrange("(k p) e -> p k e", p=P)).then_inc(s["bcload"], 16)
                if l == 0:
                    for r in range(2):
                        early = 512 * (12 - MOD_EARLY)
                        sp.dma_start(modrow[1][r:r + 1, early:6 * D], a["b_mod"][1:2, early:6 * D]).then_inc(S[1]["b_load"], 16)
                    for n in range(first_of[1] + 2, after_experts):
                        load_chunk(n)

                for q in range(2):
                    sp.wait_ge(s[f"h2st{q}"], c0[f"h2st{q}"] + 8 * len(active(l)))
                if l == 0:
                    sp.wait_ge(S[1]["modmm"], before[1]["modmm"] + MOD_EARLY)
                sp.wait_ge(s["blocks"], c0["blocks"] + 1)
                nblk = sp.value_load(meta[0:1, NBLK:NBLK + 1], min_val=1, max_val=NBLK)
                with sp.Fori(0, NBLK // 2) as i:
                    for u in range(2):
                        b = i * 2 + u
                        with sp.If(b < nblk):
                            e = sp.value_load(meta[0:1, bass.ds(b, 1)], min_val=0, max_val=NE - 1)
                            for j, w in enumerate(("w_gate", "w_up", "w_down")):
                                dst = RING[:, 3 * u + j, :]
                                if j < 2:
                                    src = a[w][l, bass.ds(e, 1), :, :].rearrange("o (k p) n -> p (o k) n", p=P)
                                    dst = dst.rearrange("p (k n) -> p k n", n=FE)
                                else:
                                    src = a[w][l, bass.ds(e, 1), :, :].rearrange("o (k p) n -> p (o k) n", p=P)
                                    dst = dst.rearrange("p (k n) -> p k n", n=D)
                                if (u, j) == (0, 1):
                                    sp.wait_ge(s["xgl0"], 16)
                                sp.wait_ge(s[("eg_mm", "eu_mm", "ed_mm")[j]], b + 1)
                                sp.dma_start(dst, src).then_inc(s[f"wl{3 * u + j}"], 16)
                sp.wait_ge(s["ed_mm"], nblk + 2)
                for st in range(2):
                    sp.dma_start(g2bc[:, st, :], mod_dram[l][st:st + 1, 5 * D:6 * D].to_broadcast([P, D])).then_inc(s["g2load"], 16)
                if l == DEPTH - 1:
                    sp.dma_start(fg, a["final_g"].rearrange("(o n) -> o n", o=1).to_broadcast([P, D])).then_inc(fin_load, 16)

            for l in range(DEPTH):
                layer(l)
            sp.wait_ge(stored, 32)

        @block.gpsimd
        def _(pool):
            for l in range(DEPTH):
                row = lambda x, n: x.rearrange("(o n) -> o n", o=1).to_broadcast([P, n])
                pool.dma_start(alog[:, l, :], row(a["a_log"][l].rearrange("d h -> (d h)"), 8)).then_inc(once["params"], 16)
                pool.dma_start(dtb[:, l, :], row(a["dt_bias"][l].rearrange("d h -> (d h)"), 8)).then_inc(once["params"], 16)
                pool.dma_start(nsink[:, l, :], row(a["sink"][l], HB)).then_inc(once["params"], 16)
                pool.dma_start(gdn_g[:, l, :], row(a["gdn_norm_g"][l], P)).then_inc(once["params"], 16)
            pool.dma_start(rbias, a["router_bias"].rearrange("(o n) -> o n", o=1).to_broadcast([P, NE])).then_inc(once["params"], 16)
            pool.memset(slot_tok[:, NBLK:NBLK + 1], 0)
            pool.memset(zero_tile, 0.0).then_inc(pool_link, 1)
            for l in range(DEPTH):
                s, c0 = S[l], before[l]
                pool.wait_ge(s["modfold"], c0["modfold"] + 2)
                pool.dma_start(mod_dram[l], modrow[l][0:2, :]).then_inc(s["modstore"], 16)
                if l == 0:
                    pool.wait_ge(pool_link, 1)
                    pool.wait_ge(s["gpre_a"], c0["gpre_a"] + 1)
                    pool.dma_start(y_dram.rearrange("(p b) (c d) -> p (b c) d", p=P, c=2),
                                   zero_tile.rearrange("p (o d) -> p o d", o=1).to_broadcast([P, 2 * NBLK, 512])).then_inc(y_zeroed, 16)
                nact = len(active(l))
                for j, t in enumerate(active(l)):
                    pool.wait_ge(s["h2row"], c0["h2row"] + j + 1)
                    pool.dma_start(h2_dram[t * P:(t + 1) * P, :], h2[:, j, :]).then_inc(s[f"h2st{j % 2}"], 16)
                pool.wait_ge(s["h2st0"], c0["h2st0"] + 8 * nact)
                pool.wait_ge(s["h2st1"], c0["h2st1"] + 8 * nact)
                pool.wait_ge(s["routed"], c0["routed"] + 1)
                nblk = pool.value_load(meta[0:1, NBLK:NBLK + 1], min_val=1, max_val=NBLK)
                pool.tensor_copy(cur_tok[:, 0:1], slot_tok[:, 0:1]).then_inc(s["idx"], 1)
                pool.wait_ge(s["idx"], 1)
                pool.indirect_dma_start(xg[:, 0, :], None, h2_dram,
                                        bass.IndirectOffsetOnAxis(cur_tok[:, 0:1], 0)).then_inc(s["xgl0"], 16)
                with pool.Fori(0, NBLK // 2) as i:
                    for u in range(2):
                        b = i * 2 + u
                        with pool.If(b < nblk):
                            v = 1 - u
                            pool.wait_ge(s["xg_mm1"], b + 2)
                            pool.wait_ge(s["routed"], c0["routed"] + 1)
                            pool.tensor_copy(cur_tok[:, v:v + 1], slot_tok[:, bass.ds(b + 1, 1)]).then_inc(s["idx"], 1)
                            pool.wait_ge(s["idx"], b + 2)
                            pool.sem_inc(pool_passed, 1)
                            pool.indirect_dma_start(xg[:, v, :], None, h2_dram,
                                                    bass.IndirectOffsetOnAxis(cur_tok[:, v:v + 1], 0)).then_inc(s[f"xgl{v}"], 16)
                pool.wait_ge(s["ed_mm"], nblk + 2)
                pool.wait_ge(s["st0"], (nblk + 1) // 2 * 16 + 16)
                pool.wait_ge(s["st1"], nblk // 2 * 16 + 16)
                pool.sem_inc(pool_passed, 1)
                for j, t in enumerate(active(l)):
                    for c in range(2):
                        pool.indirect_dma_start(yg[:, 2 * j + c, :], None, y_dram,
                                                bass.IndirectOffsetOnAxis(pos_u[:, c, t:t + 1], 0)).then_inc(s[f"ygl{j}"], 16)

        @block.tensor
        def _(pe):
            def layer(l):
                s, c0 = S[l], before[l]
                act_t = active(l)
                if l == 0:
                    pe.wait_ge(con_loaded, 16)
                    pe.wait_ge(small_loaded, 16 * (2 + DEPTH))
                    pe.transpose(bank[0][:, 0:16], crow[0:16, :], ident[0:16, 0:16])
                    for m in range(DEPTH):
                        mm = pe.transpose(bank[1][:, 64 * m:64 * m + 60], cwrow[0:60, m, :], ident[0:60, 0:60])
                    mm.then_inc(once["ct_mm"], 1)
                pe.wait_ge(once["c_silu"], 1)
                for n in range(0 if l == 0 else MOD_EARLY, 12):
                    if n == 11:
                        xn_transposes(l, (0, 1))
                    mod_chunk(l, n)
                pe.wait_ge(s["modfold"], c0["modfold"] + 2)
                for k in range(KD):
                    for j in range(2):
                        mm = pe.matmul(bank[5][:, 4 * k + 2 * j:4 * k + 2 * j + 2], modrow[l][0:2, j * D + k * P:j * D + (k + 1) * P],
                                       ident[0:2, 0:2], start=True, stop=True)
                mm.then_inc(s["modT_mm"], 1)
                xn_transposes(l, (2, 3))
                pe.wait_ge(s["xt_ev"], c0["xt_ev"] + NT)
                pe.wait_ge(s["xt_ea"], c0["xt_ea"] + NT)
                for c in range(CHT):
                    if c % 4 == 0:
                        ring_wait(pe, l, ("in", c // 4))
                    if c >= 2:
                        pe.wait_ge(s["pj_pad"], c0["pj_pad"] + c - 1)
                    w = ring(l, ("in", c // 4))
                    for k in range(KD):
                        mm = pe.matmul(bank[c % 2][:, :], w[:, k, (c % 4) * P:(c % 4 + 1) * P], HT[:, k, :],
                                       start=k == 0, stop=k == KD - 1)
                    mm.then_inc(s["pj_mm"], 1)
                groups = row_groups(l)
                for r, (c, t, (o, width, _)) in enumerate(groups):
                    if r == len(groups) - 1:
                        pe.wait_ge(s["gpre_d"], c0["gpre_d"] + 1)
                        for q in range(NT):
                            pe.matmul(bank[4][:, q * 8:q * 8 + 4], con("upper"), gg[:, q, 0:4], start=True, stop=True)
                            pe.matmul(bank[4][:, q * 8 + 4:q * 8 + 8], con("lower"), gg[:, q, 4:8], start=True, stop=True)
                            mm = pe.matmul(bank[5][:, q * 8:q * 8 + 8], con("ones"), gg[:, q, :], start=True, stop=True)
                        mm.then_inc(s["gpre_mm"], 1)
                    ring_wait(pe, l, ("in", c))
                    w = ring(l, ("in", c))
                    if r >= 2:
                        pe.wait_ge(s["row_ev"], c0["row_ev"] + r - 1)
                    for k in range(KD):
                        mm = pe.matmul(bank[2 + r % 2][:, 0:width], HT[:, k, t * P:(t + 1) * P], w[:, k, o:o + width],
                                       start=k == 0, stop=k == KD - 1)
                    mm.then_inc(s["row_mm"], 1)
                    if r < 4:
                        pe.wait_ge(s["pj_silu"], c0["pj_silu"] + 8 + r + 1)
                        transpose_rows(s, c0, TURNS.index(("v", r)), vT[:, r, :])
                    if r < 8:
                        pe.wait_ge(s["l2sq"], c0["l2sq"] + r + 1)
                        if r >= 2:
                            pe.wait_ge(s["l2ln"], c0["l2ln"] + r - 1)
                        pe.matmul(bank[4 + r % 2][:, :], con("ones"), sq[:, r % 2, :], start=True, stop=True).then_inc(s["l2mm"], 1)
                    if 2 <= r < 6:
                        pe.wait_ge(s["l2out"], c0["l2out"] + r - 1)
                        transpose_rows(s, c0, TURNS.index(("k", r - 2)), QK[:, 4 + r - 2, :])
                pe.wait_ge(s["gpre_a"], c0["gpre_a"] + 1)
                pe.wait_ge(s["tr_ev"], c0["tr_ev"] + 8)
                for g, pair in enumerate(scan):
                    gdn_group(s, c0, g, pair)
                attention(l, s, c0)
                merge(l, s, c0)
                route(l, s, c0)
                experts(l, s, c0)

            def mod_chunk(l, n):
                s, c0 = S[l], before[l]
                c = MOD_ORDER[l][n]
                banks = 2 if l else 4
                if n >= banks:
                    pe.wait_ge(s["modev"], c0["modev"] + n - banks + 1)
                o = mod_bank(l, n)
                if l:
                    pe.wait_ge(s["b_load"], c0["b_load"] + (96 if n >= MOD_EARLY else 32))
                    pe.matmul(o, ident[0:2, 0:2], modrow[l][0:2, 512 * c:512 * c + 512], start=True, stop=False)
                ring_wait(pe, l, ("mod", c))
                w = ring(l, ("mod", c))
                for k in range(KD):
                    mm = pe.matmul(o, sT[:, k, :], w[:, k, :], start=l == 0 and k == 0, stop=k == KD - 1)
                mm.then_inc(s["modmm"], 1)

            def xn_transposes(l, tiles):
                s, c0 = S[l], before[l]
                for t in tiles:
                    pe.wait_ge(s["xn"], c0["xn"] + t + 1)
                    if t >= 2:
                        pe.wait_ge(s["xt_ev"], c0["xt_ev"] + t - 1)
                        pe.wait_ge(s["xt_ea"], c0["xt_ea"] + t - 1)
                    for k in range(KD):
                        mm = pe.transpose(bank[2 * (t % 2) + k // 4][:, (k % 4) * P:(k % 4 + 1) * P],
                                          xn[l][:, t, k * P:(k + 1) * P], ident)
                    mm.then_inc(s["xt_mm"], 1)

            def transpose_rows(s, c0, n, src):
                if n >= 2:
                    pe.wait_ge(s["tr_ev"], c0["tr_ev"] + n - 1)
                for t in range(NT):
                    mm = pe.transpose(bank[6 + n % 2][:, t * P:(t + 1) * P], src[:, t * P:(t + 1) * P], ident)
                mm.then_inc(s["tr_mm"], 1)

            def gdn_group(s, c0, g, pair):
                def each(f):
                    for d, t in pair:
                        f(d, t, slice(t * P, (t + 1) * P), bank[4 * d:4 * d + 4])

                def grow(d, t, ts, bk):
                    pe.wait_ge(s[f"gd{d}"], c0[f"gd{d}"] + gv(DV_SIG, g, "gb"))
                    for h in range(HA):
                        mm = pe.matmul(bk[0][:, h * P:(h + 1) * P], gW[d][:, h, :], con("lower" if d else "upper"), start=True, stop=True)
                    mm.then_inc(s[f"gp{d}"], 1)

                def kk(d, t, ts, bk):
                    for h in range(HA):
                        pe.matmul(bk[1][:, h * P:(h + 1) * P], QK[:, 4 + h, ts], QK[:, 4 + h, ts], start=True, stop=True)
                        mm = pe.matmul(bk[2][:, h * P:(h + 1) * P], QK[:, 4 + h, ts], QK[:, h, ts], start=True, stop=True)
                    mm.then_inc(s[f"gp{d}"], 1)

                def nt(d, t, ts, bk):
                    pe.wait_ge(s[f"gd{d}"], c0[f"gd{d}"] + gv(DV_SIG, g, "n"))
                    for h in range(HA):
                        mm = pe.transpose(bk[3][:, h * P:(h + 1) * P], gN[d][:, h, :], ident)
                    mm.then_inc(s[f"gp{d}"], 1)

                each(grow)
                each(kk)
                each(nt)
                for k in range(1, LV):
                    def w(d, t, ts, bk):
                        if k > 1:
                            pe.wait_ge(s[f"ga{d}"], c0[f"ga{d}"] + gv(AC_SIG, g, f"y{k - 1}"))
                        else:
                            pe.wait_ge(s[f"gd{d}"], c0[f"gd{d}"] + gv(DV_SIG, g, "lvl0"))
                        lt = gN[d] if d else gNT[d]
                        for h in range(HA):
                            mm = pe.matmul(bk[0][:, h * P:(h + 1) * P], lt[:, h, :], gY[d][:, h, :], start=True, stop=True)
                        mm.then_inc(s[f"gp{d}"], 1)

                    def y(d, t, ts, bk):
                        pe.wait_ge(s[f"gd{d}"], c0[f"gd{d}"] + gv(DV_SIG, g, f"w{k}"))
                        if k < LV - 1 or d:
                            for h in range(HA):
                                mm = pe.matmul(bk[1][:, h * P:(h + 1) * P], gYT[d][:, h, :], gW[d][:, h, :], start=True, stop=True)
                            mm.then_inc(s[f"gp{d}"], 1)
                        if k < LV - 1 or not d:
                            for h in range(HA):
                                mm = pe.matmul(bk[2][:, h * P:(h + 1) * P], gW[d][:, h, :], gYT[d][:, h, :], start=True, stop=True)
                            mm.then_inc(s[f"gp{d}"], 1)
                    each(w)
                    each(y)

                def ks(d, t, ts, bk):
                    if g:
                        pe.wait_ge(s[f"gd{d}"], c0[f"gd{d}"] + g * len(DV_SIG))
                    for h in range(HA):
                        mm = pe.matmul(bk[0][:, h * P:(h + 1) * P], QK[:, 4 + h, ts], state[:, 4 * d + h, :], start=True, stop=True)
                    mm.then_inc(s[f"gp{d}"], 1)

                def xr(d, t, ts, bk):
                    pe.wait_ge(s[f"gd{d}"], c0[f"gd{d}"] + gv(DV_SIG, g, "r"))
                    inv = gY[d] if d else gYT[d]
                    for h in range(HA):
                        mm = pe.matmul(bk[3][:, h * P:(h + 1) * P], inv[:, h, :], gN[d][:, h, :], start=True, stop=True)
                    mm.then_inc(s[f"gp{d}"], 1)

                def qs(d, t, ts, bk):
                    pe.wait_ge(s[f"ga{d}"], c0[f"ga{d}"] + gv(AC_SIG, g, "vn"))
                    for h in range(HA):
                        pe.matmul(bk[1][:, h * P:(h + 1) * P], QK[:, h, ts], state[:, 4 * d + h, :], start=True, stop=True)
                        mm = pe.matmul(bk[2][:, h * P:(h + 1) * P], gAt[d][:, h, :], gNT[d][:, h, :], start=True, stop=True)
                    mm.then_inc(s[f"gp{d}"], 1)

                def kv(d, t, ts, bk):
                    pe.wait_ge(s[f"gd{d}"], c0[f"gd{d}"] + gv(DV_SIG, g, "vs"))
                    for h in range(HA):
                        mm = pe.matmul(bk[0][:, h * P:(h + 1) * P], krow[:, t, h * P:(h + 1) * P], gE[d][:, h, :], start=True, stop=True)
                    mm.then_inc(s[f"gp{d}"], 1)
                each(ks)
                each(xr)
                each(qs)
                each(kv)

            def attention(l, s, c0):
                for d in range(2):
                    pe.wait_ge(s[f"gd{d}"], c0[f"gd{d}"] + len(scan) * len(DV_SIG))
                for t in range(NT):
                    pe.transpose(bank[0][:, t * P:(t + 1) * P], arow[:, t, A_K:A_K + P], ident)
                    mm = pe.transpose(bank[1][:, t * P:(t + 1) * P], kswap[:, t, :], ident)
                mm.then_inc(s["kt_mm"], 1)
                for j, t in enumerate(active(l)):
                    for m in range(4):
                        mm = pe.transpose(bank[2 + j][:, m * P:(m + 1) * P], arow[:, t, A_Q + m * P:A_Q + (m + 1) * P], ident)
                    mm.then_inc(s["kt_mm"], 1)
                pe.wait_ge(s["kt_ev"], c0["kt_ev"] + 1 + len(active(l)))
                units = att_units(l)
                for n in range(len(units) + 2):
                    if n < len(units):
                        j, t, h, keys, _ = units[n]
                        if n >= 2:
                            pe.wait_ge(s["at_p"], c0["at_p"] + n - 1)
                        o, g = h % 2, h // (HB // GB)
                        kt = kTA if g == o else kTB
                        rows = slice(64 * o, 64 * o + 64)
                        pe.matmul(bank[n % 2][:, 0:keys], qT[rows, t, (h // 2) * P:(h // 2 + 1) * P], kt[rows, 0:keys],
                                  start=True, stop=True).then_inc(s["at_s"], 1)
                    if 1 <= n <= len(units):
                        m = n - 1
                        pe.wait_ge(s["at_p"], c0["at_p"] + m + 1)
                        if m >= 2:
                            pe.wait_ge(s["at_tev"], c0["at_tev"] + m - 1)
                        for q in range(units[m][3] // P):
                            mm = pe.transpose(bank[2 + m % 2][:, q * P:(q + 1) * P], prob[:, m % 2, q * P:(q + 1) * P], ident)
                        mm.then_inc(s["at_tr"], 1)
                    if n >= 2:
                        m = n - 2
                        j, t, h, keys, _ = units[m]
                        nk = keys // P
                        pe.wait_ge(s["at_tev"], c0["at_tev"] + m + 1)
                        if h == 0 and j >= 2:
                            pe.wait_ge(s["at_y"], c0["at_y"] + j - 1)
                        for q in range(nk):
                            mm = pe.matmul(bank[4 + j % 2][:, h * DH:(h + 1) * DH], probT[:, m % 2, q * P:(q + 1) * P],
                                           arow[:, q, A_V + (h // 4) * DH:A_V + (h // 4 + 1) * DH], start=q == 0, stop=q == nk - 1)
                        mm.then_inc(s["at_o"], 1)

            def merge(l, s, c0):
                act_t = active(l)
                n = 0
                for src, sem in ((orow, "o_ya"), (yb, "at_y")):
                    pe.wait_ge(s[sem], c0[sem] + len(act_t))
                    for t in act_t:
                        if n >= 2:
                            pe.wait_ge(s["mT_ev"], c0["mT_ev"] + n - 1)
                        for k in range(4):
                            mm = pe.transpose(bank[6 + n % 2][:, k * P:(k + 1) * P], src[:, t, k * P:(k + 1) * P], ident)
                        mm.then_inc(s["mT_mm"], 1)
                        n += 1
                pe.wait_ge(s["mT_ev"], c0["mT_ev"] + n)
                n = 0
                for half in range(2):
                    for step in range(4):
                        key = (f"m{min(step, 2)}", half)
                        ring_wait(pe, l, key)
                        w = ring(l, key)
                        lhs, k0, nk = ((HT, 0, KD), (HT, 0, KD), (yaT, 0, 4), (ybT, 4, 4))[step]
                        for t in act_t:
                            if n >= 8:
                                name, v = merge_evac(l, n - 8)
                                pe.wait_ge(s[name], c0[name] + v)
                            for k in range(nk):
                                mm = pe.matmul(bank[n % 8][:, :], lhs[:, k, t * P:(t + 1) * P], w[:, k0 + k, :], start=k == 0, stop=k == nk - 1)
                            mm.then_inc(s["mg_mm"], 1)
                            n += 1
                pe.wait_ge(s["mg_d"], c0["mg_d"] + 4 * len(act_t))
                for j, t in enumerate(act_t):
                    if j >= 2:
                        pe.wait_ge(s["m2_ev"], c0["m2_ev"] + 2 * (j - 1))
                    for k in range(KD):
                        mm = pe.transpose(bank[2 * (j % 2) + k // 4][:, (k % 4) * P:(k % 4 + 1) * P], mrow[:, t, k * P:(k + 1) * P], ident)
                        if k % 4 == 3:
                            mm.then_inc(s["m2_mm"], 1)
                pe.wait_ge(s["m2_ev"], c0["m2_ev"] + 2 * len(act_t))
                n = 0
                for half in range(2):
                    ring_wait(pe, l, ("o", half))
                    w = ring(l, ("o", half))
                    for t in act_t:
                        if n >= 2:
                            pe.wait_ge(s["y_ev"], c0["y_ev"] + n - 1)
                        for k in range(KD):
                            mm = pe.matmul(bank[4 + n % 2][:, :], HT[:, k, t * P:(t + 1) * P], w[:, k, :], start=k == 0, stop=k == KD - 1)
                        mm.then_inc(s["y_mm"], 1)
                        n += 1

            def route(l, s, c0):
                act_t = active(l)
                early = list(range(MOD_EARLY)) if l == 0 else []
                for n in early[0:2]:
                    mod_chunk(l + 1, n)
                pe.wait_ge(s["bcload"], c0["bcload"] + 80)
                for j in range(len(act_t) + 1):
                    if j < len(act_t):
                        pe.wait_ge(s["h2row"], c0["h2row"] + j + 1)
                        if j >= 2:
                            pe.wait_ge(s["r_tev"], c0["r_tev"] + j - 1)
                        for k in range(KD):
                            mm = pe.transpose(bank[4 * (j % 2) + k // 4][:, (k % 4) * P:(k % 4 + 1) * P], h2[:, j, k * P:(k + 1) * P], ident)
                        mm.then_inc(s["r_tr"], 1)
                    if j == 1:
                        for n in early[2:3]:
                            mod_chunk(l + 1, n)
                    if j >= 1:
                        q = j - 1
                        pe.wait_ge(s["r_tev"], c0["r_tev"] + q + 1)
                        for k in range(KD):
                            mm = pe.matmul(bank[2][:, q * NE:(q + 1) * NE], h2T[:, q % 2, k * P:(k + 1) * P], wr[:, k, :],
                                           start=k == 0, stop=k == KD - 1)
                        mm.then_inc(s["r_mm"], 1)
                for n in early[3:6]:
                    mod_chunk(l + 1, n)
                pe.wait_ge(s["r_hot"], c0["r_hot"] + 1)
                nact = len(act_t)
                hot = rt[5]
                for j in range(nact):
                    o = bank[3][:, j * NE:(j + 1) * NE]
                    for q in range(j):
                        pe.matmul(o, con("ones"), hot[:, q, :], start=q == 0, stop=False)
                    pe.matmul(o, con("supper"), hot[:, j, :], start=j == 0, stop=True)
                for q in range(nact):
                    mm = pe.matmul(bank[4][:, 0:NE], con("ones"), hot[:, q, :], start=q == 0, stop=q == nact - 1)
                mm.then_inc(s["r_rank"], 1)
                for n in early[6:8]:
                    mod_chunk(l + 1, n)
                for name in ("xg_mm1", "eg_mm", "eu_mm", "ed_mm"):
                    pe.sem_inc(s[name], 2)
                pe.wait_ge(s["r_sort"], c0["r_sort"] + 1)
                for q in range(2 * nact):
                    mm = pe.matmul(bank[5][:, 0:NBLK], hot_r[:, q, :], hot_b[:, q, :], start=q == 0, stop=q == 2 * nact - 1)
                mm.then_inc(s["r_inv"], 1)

            def experts(l, s, c0):
                pe.wait_ge(s["routed"], c0["routed"] + 1)
                nblk = pe.value_load(meta[0:1, NBLK:NBLK + 1], min_val=1, max_val=NBLK)
                def turn(half, u):
                    for k in range(4 * half, 4 * half + 4):
                        mm = pe.transpose(bank[half][:, (k % 4) * P:(k % 4 + 1) * P], xg[:, u, k * P:(k + 1) * P], ident)
                    mm.then_inc(s[f"xg_mm{half}"], 1)

                pe.wait_ge(s["xgl0"], 16)
                turn(0, 0)
                turn(1, 0)
                with pe.Fori(0, NBLK // 2) as i:
                    for u in range(2):
                        b = i * 2 + u
                        with pe.If(b < nblk):
                            wg = RING[:, 3 * u, :].rearrange("p (k n) -> p k n", n=FE)
                            wu = RING[:, 3 * u + 1, :].rearrange("p (k n) -> p k n", n=FE)
                            wd = RING[:, 3 * u + 2, :].rearrange("p (k n) -> p k n", n=D)
                            pe.wait_ge(s["xg_ev0"], b + 1)
                            pe.wait_ge(s["xg_ev1"], b + 1)
                            pe.wait_ge(s[f"wl{3 * u}"], (i + 1) * 16)
                            for k in range(KD):
                                mm = pe.matmul(bank[2][:, :], xT[:, u, k * P:(k + 1) * P], wg[:, k, :], start=k == 0, stop=k == KD - 1)
                            mm.then_inc(s["eg_mm"], 1)
                            pe.wait_ge(s[f"wl{3 * u + 1}"], (i + 1) * 16)
                            for k in range(KD):
                                mm = pe.matmul(bank[3][:, :], xT[:, u, k * P:(k + 1) * P], wu[:, k, :], start=k == 0, stop=k == KD - 1)
                            mm.then_inc(s["eu_mm"], 1)
                            pe.wait_ge(s[f"xgl{1 - u}"], (i + 1 + u) * 16)
                            turn(0, 1 - u)
                            pe.wait_ge(s["e_he"], b + 1)
                            for k in range(KF):
                                mm = pe.transpose(bank[4][:, k * P:(k + 1) * P], he[:, u, k * P:(k + 1) * P], ident)
                            mm.then_inc(s["ht_mm"], 1)
                            turn(1, 1 - u)
                            pe.wait_ge(s["ht_ev"], b + 1)
                            pe.wait_ge(s["ed_ev0"], b + 1)
                            pe.wait_ge(s["ed_ev1"], b + 1)
                            pe.wait_ge(s[f"wl{3 * u + 2}"], (i + 1) * 16)
                            for n in range(2):
                                for k in range(KF):
                                    mm = pe.matmul(bank[5 + n][:, :], heT[:, u, k * P:(k + 1) * P], wd[:, k, n * 512:(n + 1) * 512],
                                                   start=k == 0, stop=k == KF - 1)
                            mm.then_inc(s["ed_mm"], 1)

            for l in range(DEPTH):
                layer(l)

        @block.scalar
        def _(act):
            n_link = [0]

            def link(ins):
                n_link[0] += 1
                ins.then_inc(act_link, 1)
                act.wait_ge(act_link, n_link[0])

            def layer(l):
                s, c0 = S[l], before[l]
                act_t = active(l)
                if l == 0:
                    act.wait_ge(once["c_T"], 1)
                    act.activation(sT[:, :, :], crow_T[:, :, :], ACT.Silu).then_inc(once["c_silu"], 1)
                if l == 0:
                    act.wait_ge(x_loaded, 32)
                for t in range(NT):
                    if l and t != 2:
                        mod_out(l, (MOD_EARLY + (t + 1) // 2,))
                    if l:
                        act.wait_ge(S[l - 1]["comb"], before[l - 1]["comb"] + t + 1)
                    link(act.activation(nsq[l], X[:, t, :], ACT.Square, accum_out=ss[:, t:t + 1]))
                link(act.activation(st1[:, 0:NT], ss[:, 0:NT], ACT.Ln, scale=1.0 / D, bias=con("eps")))
                act.activation(rstd[:, 0:NT], st1[:, 0:NT], ACT.Exp, scale=-0.5).then_inc(s["rs0"], 1)
                if l:
                    mod_out(l, (11,))
                act.wait_ge(s["modT_ev"], c0["modT_ev"] + 1)
                for t in range(NT):
                    act.wait_ge(s["xt_mm"], c0["xt_mm"] + t + 1)
                    for k in range(4, KD):
                        last = act.activation(HT[:, k, t * P:(t + 1) * P], bank[2 * (t % 2) + 1][:, (k - 4) * P:(k - 3) * P],
                                              ACT.Identity, scale=modT[:, k, 2 + stream(t):3 + stream(t)],
                                              bias=modT[:, k, stream(t):stream(t) + 1])
                    last.then_inc(s["xt_ea"], 1)
                for c in range(CHT + 1):
                    if c < CHT:
                        act.wait_ge(s["pj_mm"], c0["pj_mm"] + c + 1)
                        act.wait_ge(zeroed, l + 1) if c == 0 else None
                        if c >= 2:
                            act.wait_ge(s["pj_conv"], c0["pj_conv"] + c - 1)
                        dst = cpad[:, c % 2, :].rearrange("p (s n) -> p s n", s=2)[:, :, 2:2 + SEQ]
                        act.copy(dst, bank[c % 2][:, :].rearrange("p (s n) -> p s n", s=2)).then_inc(s["pj_pad"], 1)
                    if c >= 1:
                        d = c - 1
                        act.wait_ge(s["pj_conv"], c0["pj_conv"] + d + 1)
                        if d == 0:
                            act.wait_ge(s["modstore"], c0["modstore"] + 16)
                        dst = QK[:, d, :] if d < 8 else vT[:, d - 8, :]
                        act.activation(dst, cy[:, d % 2, :], ACT.Silu).then_inc(s["pj_silu"], 1)
                groups = row_groups(l)
                act.wait_ge(s["pj_silu"], c0["pj_silu"] + 12)
                act.activation(sq[:, 0, :], QK[:, L2_ORDER[0], :], ACT.Square).then_inc(s["l2sq"], 1)
                for r, (c, t, (o, width, dcol)) in enumerate(groups):
                    if r == 8:
                        decays(l, s, c0)
                    act.wait_ge(s["row_mm"], c0["row_mm"] + r + 1)
                    if c == 3:
                        act.activation(zrow[:, t, :], bank[2 + r % 2][:, 0:512], ACT.Silu).then_inc(s["row_ev"], 1)
                    else:
                        act.copy(arow[:, t, dcol:dcol + width], bank[2 + r % 2][:, 0:width]).then_inc(s["row_ev"], 1)
                    if r < 8:
                        act.wait_ge(s["l2mm"], c0["l2mm"] + r + 1)
                        if r >= 2:
                            act.wait_ge(s["l2out"], c0["l2out"] + r - 1)
                        link(act.activation(cy[:, r % 2, :], bank[4 + r % 2][:, :], ACT.Ln, bias=con("eps")))
                        act.activation(cy[:, r % 2, :], cy[:, r % 2, :], ACT.Exp, scale=-0.5).then_inc(s["l2ln"], 1)
                    if r < 7:
                        act.activation(sq[:, (r + 1) % 2, :], QK[:, L2_ORDER[r + 1], :], ACT.Square).then_inc(s["l2sq"], 1)
                act.wait_ge(s["gpre_z"], c0["gpre_z"] + 1)
                act.activation(eg[:, :, :], gcum[:, :, :], ACT.Exp)
                act.activation(egt[:, :, :], gtot[:, :, :], ACT.Exp)
                act.activation(ek[:, :, :], ek[:, :, :], ACT.Exp).then_inc(s["gpre_e"], 1)
                for g, pair in enumerate(scan):
                    for d, t in pair:
                        act.wait_ge(s[f"gd{d}"], c0[f"gd{d}"] + gv(DV_SIG, g, "clamp"))
                        act.activation(gE[d][:, :, :], gE[d][:, :, :], ACT.Exp, scale=-1.0)
                        act.activation(gAt[d][:, :, :], gAt[d][:, :, :], ACT.Exp).then_inc(s[f"ga{d}"], 1)
                    for d, t in pair:
                        act.wait_ge(s[f"gp{d}"], c0[f"gp{d}"] + gv(PE_SIG, g, "nt"))
                        act.copy(gNT[d][:, :, :], heads(bank[4 * d + 3])).then_inc(s[f"ga{d}"], 1)
                    for k in range(1, LV - 1):
                        for d, t in pair:
                            act.wait_ge(s[f"gp{d}"], c0[f"gp{d}"] + gv(PE_SIG, g, f"y{k}"))
                            act.copy(gY[d][:, :, :], heads(bank[4 * d + 1])).then_inc(s[f"ga{d}"], 1)
                    for d, t in pair:
                        act.wait_ge(s[f"gp{d}"], c0[f"gp{d}"] + gv(PE_SIG, g, "xr"))
                        act.copy(gNT[d][:, :, :], heads(bank[4 * d + 3])).then_inc(s[f"ga{d}"], 1)
                for n, (j, t, h, keys, _) in enumerate(att_units(l)):
                    if n == 2:
                        act.wait_ge(s["o_sq"], c0["o_sq"] + 1)
                        nn = 4 * len(act_t)
                        link(act.activation(st1[:, 0:nn], ss[:, 0:nn], ACT.Ln, scale=1.0 / P, bias=con("eps")))
                        act.activation(rstd[:, 0:nn], st1[:, 0:nn], ACT.Exp, scale=-0.5).then_inc(s["o_rs"], 1)
                    act.wait_ge(s["at_nm"], c0["at_nm"] + n + 1)
                    if n >= 2:
                        act.wait_ge(s["at_tr"], c0["at_tr"] + n - 1)
                    act.activation(esk[:, t, h:h + 1], nsink[:, l, h:h + 1], ACT.Exp, scale=-1.0, bias=nm[:, t, h:h + 1])
                    act.activation(prob[:, n % 2, 0:keys], bank[n % 2][:, 0:keys], ACT.Exp, scale=SCALE, bias=nm[:, t, h:h + 1],
                                   accum_out=den[:, t, h:h + 1]).then_inc(s["at_p"], 1)
                nact = len(act_t)
                for half in range(2):
                    for step, dst in enumerate((ga, gb)):
                        for j in range(nact):
                            n = (4 * half + step) * nact + j
                            act.wait_ge(s["mg_mm"], c0["mg_mm"] + n + 1)
                            if half:
                                act.wait_ge(s["mg_d"], c0["mg_d"] + step * nact + j + 1)
                            act.activation(dst[:, j, :], bank[n % 8][:, :], ACT.Exp, scale=-1.0).then_inc(s["mg_a"], 1)
                for j, t in enumerate(act_t):
                    act.wait_ge(s["y_ev"], c0["y_ev"] + len(act_t) + j + 1)
                    link(act.activation(h2sq, X[:, t, :], ACT.Square, accum_out=ss[:, j:j + 1]))
                nn = len(act_t)
                link(act.activation(st1[:, 0:nn], ss[:, 0:nn], ACT.Ln, scale=1.0 / D, bias=con("eps")))
                act.activation(rstd[:, 0:nn], st1[:, 0:nn], ACT.Exp, scale=-0.5).then_inc(s["n2rs0"], 1)
                if l == 0:
                    mod_out(l + 1, range(3))
                act.wait_ge(s["r_mm"], c0["r_mm"] + nn)
                act.activation(rt[0][:, 0:nn, :], bank[2][:, 0:nn * NE].rearrange("p (t e) -> p t e", e=NE), ACT.Exp,
                               scale=-1.0).then_inc(s["r_a"], 1)
                if l == 0:
                    mod_out(l + 1, range(3, MOD_EARLY))
                act.wait_ge(s["routed"], c0["routed"] + 1)
                act.wait_ge(y_zeroed, 16)
                nblk = act.value_load(meta[0:1, NBLK:NBLK + 1], min_val=1, max_val=NBLK)
                act.sem_inc(s["ed_ev1"], 1)
                act.wait_ge(s["xg_mm1"], 3)
                act.copy(xT[:, 0, 512:1024], bank[1][:, :]).then_inc(s["xg_ev1"], 1)
                act.sem_inc(s["st0"], 16)
                act.sem_inc(s["st1"], 16)
                with act.Fori(0, NBLK // 2) as i:
                    for u in range(2):
                        b = i * 2 + u
                        with act.If(b < nblk):
                            act.wait_ge(s["eg_mm"], b + 3)
                            act.activation(eg_s[:, u, :], bank[2][:, :], ACT.Silu).then_inc(s["e_silu"], 1)
                            act.wait_ge(s["ht_mm"], b + 1)
                            act.copy(heT[:, u, :], bank[4][:, :]).then_inc(s["ht_ev"], 1)
                            act.wait_ge(s["xg_mm1"], b + 4)
                            act.copy(xT[:, 1 - u, 512:1024], bank[1][:, :]).then_inc(s["xg_ev1"], 1)
                            act.wait_ge(s[f"st{u}"], (i + 1) * 16)
                            act.wait_ge(s["ed_mm"], b + 3)
                            act.copy(yrow[:, u, 512:1024], bank[6][:, :]).then_inc(s["ed_ev1"], 1)
                            act.wait_ge(s["ed_ev1"], b + 2)
                            act.wait_ge(s["ed_ev0"], b + 2)
                            act.dma_start(y_dram[bass.ds(b * P, P), :], yrow[:, u, :]).then_inc(s[f"st{u}"], 16)
                if l == DEPTH - 1:
                    act.wait_ge(s["comb"], c0["comb"] + 2)
                    for j, t in enumerate(act_t):
                        link(act.activation(fsq, X[:, t, :], ACT.Square, accum_out=ss[:, j:j + 1]))
                    link(act.activation(st1[:, 0:2], ss[:, 0:2], ACT.Ln, scale=1.0 / D, bias=con("eps")))
                    act.activation(rstd[:, 0:2], st1[:, 0:2], ACT.Exp, scale=-0.5).then_inc(once["f_rs"], 1)
                    for j, t in enumerate(act_t):
                        act.wait_ge(once["f_out"], j + 1)
                        act.dma_start(out[0, j * P:(j + 1) * P, :], X[:, t, :]).then_inc(stored, 16)

            def mod_out(l, chunk_numbers):
                s, c0 = S[l], before[l]
                for n in chunk_numbers:
                    act.wait_ge(s["modmm"], c0["modmm"] + n + 1)
                    c = MOD_ORDER[l][n]
                    act.copy(modrow[l][0:2, 512 * c:512 * c + 512], mod_bank(l, n)).then_inc(s["modev"], 1)

            def decays(l, s, c0):
                act.wait_ge(s["row_ev"], c0["row_ev"] + 4)
                link(act.activation(bt[:, :, :], arow[:, :, 0:8], ACT.Exp, scale=-1.0))
                act.wait_ge(once["params"], 16 * (4 * DEPTH + 1))
                link(act.activation(nbeta[:, 0, :], alog[:, l, :], ACT.Exp))
                act.wait_ge(s["gpre_x"], c0["gpre_x"] + 1)
                link(act.activation(gcum[:, :, :], gcum[:, :, :], ACT.Exp, scale=-1.0))
                act.activation(gcum[:, :, :], gcum[:, :, :], ACT.Ln, bias=1.0).then_inc(s["gpre_y"], 1)

            for l in range(DEPTH):
                layer(l)

        @block.vector
        def _(dve):
            n_link = [0]

            def link(ins):
                n_link[0] += 1
                ins.then_inc(dve_link, 1)
                dve.wait_ge(dve_link, n_link[0])

            def newton(n, inv_width):
                link(dve.tensor_scalar(st1[:, 0:n], ss[:, 0:n], inv_width, EPS, ALU.mult, ALU.add))
                link(dve.tensor_tensor(st2[:, 0:n], rstd[:, 0:n], rstd[:, 0:n], ALU.mult))
                link(dve.tensor_tensor(st2[:, 0:n], st2[:, 0:n], st1[:, 0:n], ALU.mult))
                link(dve.tensor_scalar(st2[:, 0:n], st2[:, 0:n], -0.5, 1.5, ALU.mult, ALU.add))
                link(dve.tensor_tensor(rstd[:, 0:n], rstd[:, 0:n], st2[:, 0:n], ALU.mult))

            def mod_bias(chunk_numbers):
                s = S[0]
                for n in chunk_numbers:
                    sl = modrow[0][0:2, 512 * n:512 * n + 512]
                    dve.wait_ge(s["modmm"], n + 1)
                    dve.tensor_tensor(sl, mod_bank(0, n), sl, ALU.add).then_inc(s["modev"], 1)

            def fold(l, j):
                sl = modrow[l][0:2, (1, 4)[j] * D:(2, 5)[j] * D]
                dve.scalar_tensor_tensor(out=sl, in0=sl, scalar=1.0, in1=gnorm[l][j][0:2, :], op0=ALU.add, op1=ALU.mult).then_inc(S[l]["modfold"], 1)

            def layer(l):
                s, c0 = S[l], before[l]
                act_t = active(l)
                if l == 0:
                    dve.wait_ge(once["ct_mm"], 1)
                    link(dve.tensor_copy(convT[:, 0, :], bank[1][:, 0:60]))
                    link(dve.tensor_copy(convT[:, 1, :], bank[1][:, 64:124]))
                    dve.tensor_copy(crow_T[:, :, :], bank[0][:, 0:16].rearrange("p (s k) -> p k s", s=2)).then_inc(once["c_T"], 1)
                if l == 0:
                    dve.wait_ge(s["b_load"], c0["b_load"] + 96)
                    mod_bias(range(8))
                    dve.wait_ge(once["params"], 16 * (4 * DEPTH + 1))
                    link(dve.tensor_scalar(nsink[:, :, :], nsink[:, :, :], -1.0, None, ALU.mult))
                    mod_bias(range(8, 9))
                dve.wait_ge(s["rs0"], c0["rs0"] + 1)
                newton(NT, 1.0 / D)
                for t in range(NT):
                    dve.tensor_scalar(xn[l][:, t, :], X[:, t, :], rstd[:, t:t + 1], None, ALU.mult).then_inc(s["xn"], 1)
                if l == 0:
                    mod_bias(range(9, 12))
                else:
                    dve.wait_ge(s["b_load"], c0["b_load"] + 128)
                dve.wait_ge(s["modev"], c0["modev"] + 12)
                fold(l, 0)
                if l == 0:
                    fold(l, 1)
                dve.wait_ge(s["modT_mm"], c0["modT_mm"] + 1)
                dve.tensor_copy(modT[:, :, :], bank[5][:, 0:32].rearrange("p (k m) -> p k m", m=4)).then_inc(s["modT_ev"], 1)
                dve.wait_ge(s["modT_ev"], c0["modT_ev"] + 1)
                for t in range(NT):
                    dve.wait_ge(s["xt_mm"], c0["xt_mm"] + t + 1)
                    for k in range(4):
                        last = dve.tensor_scalar(HT[:, k, t * P:(t + 1) * P], bank[2 * (t % 2)][:, k * P:(k + 1) * P],
                                                 modT[:, k, 2 + stream(t):3 + stream(t)], modT[:, k, stream(t):stream(t) + 1],
                                                 ALU.mult, ALU.add)
                    last.then_inc(s["xt_ev"], 1)
                dve.memset(cpad[:, :, :], 0.0).then_inc(zeroed, 1)
                for c in range(CHT):
                    dve.wait_ge(s["pj_pad"], c0["pj_pad"] + c + 1)
                    if c >= 2:
                        dve.wait_ge(s["pj_silu"], c0["pj_silu"] + c - 1)
                    src = cpad[:, c % 2, :].rearrange("p (s n) -> p s n", s=2)
                    dst = cy[:, c % 2, :].rearrange("p (s n) -> p s n", s=2)
                    link(dve.tensor_scalar(dst, src[:, :, 0:SEQ], convT[:, l, c:c + 1], None, ALU.mult))
                    for j in range(1, CONV):
                        ins = dve.scalar_tensor_tensor(out=dst, in0=src[:, :, j:j + SEQ], scalar=convT[:, l, j * CHT + c:j * CHT + c + 1],
                                                       in1=dst, op0=ALU.mult, op1=ALU.add)
                        if j < CONV - 1:
                            link(ins)
                        else:
                            ins.then_inc(s["pj_conv"], 1)
                for r in range(8):
                    c = L2_ORDER[r]
                    for kind, h in turns_at(r)[:1] if r < 4 else ():
                        row_copy(s, c0, kind, h)
                    dve.wait_ge(s["l2ln"], c0["l2ln"] + r + 1)
                    dve.scalar_tensor_tensor(out=QK[:, c, :], in0=QK[:, c, :], scalar=float(P) ** -0.5 if c < 4 else 1.0,
                                             in1=cy[:, r % 2, :], op0=ALU.mult, op1=ALU.mult).then_inc(s["l2out"], 1)
                    if 2 <= r < 6:
                        row_copy(s, c0, "k", r - 2)
                dve.wait_ge(s["row_ev"], c0["row_ev"] + 8)
                per_tile = lambda v: v[:, l, :].rearrange("p (o h) -> p o h", o=1).to_broadcast([P, NT, 8])
                link(dve.tensor_tensor(gg[:, :, :], arow[:, :, 8:16], per_tile(dtb), ALU.add))
                link(dve.tensor_scalar(gtot[:, :, :], gg[:, :, :], -1.0, None, ALU.mult))
                dve.tensor_tensor(gcum[:, :, :], gg[:, :, :], gtot[:, :, :], ALU.max).then_inc(s["gpre_x"], 1)
                dve.wait_ge(s["gpre_y"], c0["gpre_y"] + 1)
                link(dve.tensor_scalar(beta[:, :, :], bt[:, :, :], 1.0, None, ALU.add))
                link(dve.reciprocal(beta[:, :, :], beta[:, :, :]))
                link(dve.tensor_scalar(gg[:, :, :], gg[:, :, :], 0.0, None, ALU.max))
                link(dve.tensor_tensor(gg[:, :, :], gg[:, :, :], gcum[:, :, :], ALU.add))
                ea = nbeta[:, 0, :].rearrange("p (o h) -> p o h", o=1).to_broadcast([P, NT, 8])
                dve.scalar_tensor_tensor(out=gg[:, :, :], in0=gg[:, :, :], scalar=-1.0, in1=ea, op0=ALU.mult, op1=ALU.mult).then_inc(s["gpre_d"], 1)
                rope()
                dve.wait_ge(s["gpre_d"], c0["gpre_d"] + 1)
                dve.wait_ge(s["gpre_mm"], c0["gpre_mm"] + 1)
                link(dve.tensor_copy(gcum[:, :, :], bank[4][:, 0:32].rearrange("p (t h) -> p t h", h=8)))
                link(dve.tensor_copy(gtot[:, :, :], bank[5][:, 0:32].rearrange("p (t h) -> p t h", h=8)))
                dve.tensor_tensor(ek[:, :, :], gtot[:, :, :], gcum[:, :, :], ALU.subtract).then_inc(s["gpre_z"], 1)
                link(dve.tensor_scalar(nbeta[:, :, :], beta[:, :, :], -1.0, None, ALU.mult))
                dve.wait_ge(s["gpre_e"], c0["gpre_e"] + 1)
                link(dve.tensor_tensor(nbg[:, :, :], nbeta[:, :, :], eg[:, :, :], ALU.mult))
                link(dve.memset(state[:, :, :], 0.0))
                dve.memset(orow[:, :, :], 0.0).then_inc(s["gpre_a"], 1)
                dve.wait_ge(s["gpre_a"], c0["gpre_a"] + 1)
                for g, pair in enumerate(scan):
                    gdn_group(s, c0, g, pair)
                attention(l, s, c0)
                merge(l, s, c0)
                norm2(l, s, c0)
                route(l, s, c0)
                experts(l, s, c0)
                combine(l, s, c0)

            def gdn_group(s, c0, g, pair):
                def sig(d, ins):
                    ins.then_inc(s[f"gd{d}"], 1)

                def mine(d, name):
                    dve.wait_ge(s[f"gd{d}"], c0[f"gd{d}"] + gv(DV_SIG, g, name))

                for d, t in pair:
                    sig(d, dve.tensor_copy(gW[d][:, :, :], per_row(gg, t, 4 * d, HA)))
                for d, t in pair:
                    dve.wait_ge(s[f"gp{d}"], c0[f"gp{d}"] + gv(PE_SIG, g, "grow"))
                    link(dve.tensor_tensor(gN[d][:, :, :], heads(bank[4 * d]), per_row(gcum, t, 4 * d, HA), ALU.subtract))
                    link(dve.tensor_scalar(gE[d][:, :, :], gN[d][:, :, :], 0.0, None, ALU.max))
                    sig(d, dve.tensor_scalar(gAt[d][:, :, :], gN[d][:, :, :], 0.0, None, ALU.min))
                for d, t in pair:
                    dve.wait_ge(s[f"ga{d}"], c0[f"ga{d}"] + gv(AC_SIG, g, "exp"))
                    link(dve.tensor_tensor(gE[d][:, :, :], gE[d][:, :, :], per_mat(con("supper" if d else "slower")), ALU.mult))
                    link(dve.tensor_tensor(gE[d][:, :, :], gE[d][:, :, :], per_row(nbeta, t, 4 * d, HA), ALU.mult))
                    dve.wait_ge(s[f"gp{d}"], c0[f"gp{d}"] + gv(PE_SIG, g, "kk"))
                    link(dve.tensor_tensor(gN[d][:, :, :], heads(bank[4 * d + 1]), gE[d][:, :, :], ALU.mult))
                    sig(d, dve.tensor_tensor(gN[d][:, :, :], gN[d][:, :, :], per_mat(ident), ALU.add))
                for d, t in pair:
                    link(dve.tensor_tensor(gAt[d][:, :, :], gAt[d][:, :, :], per_mat(con("lower" if d else "upper")), ALU.mult))
                    sig(d, dve.tensor_tensor(gAt[d][:, :, :], heads(bank[4 * d + 2]), gAt[d][:, :, :], ALU.mult))
                for d, t in pair:
                    dve.wait_ge(s[f"ga{d}"], c0[f"ga{d}"] + gv(AC_SIG, g, "nt"))
                    mine(d, "n")
                    low, lowT = (gNT, gN) if d else (gN, gNT)
                    dve.tensor_tensor(gY[d][:, :, :], low[d][:, :, :], per_mat(con("level0")), ALU.mult)
                    sig(d, dve.tensor_tensor(gYT[d][:, :, :], lowT[d][:, :, :], per_mat(con("level0T")), ALU.mult))
                for k in range(1, LV):
                    for d, t in pair:
                        dve.wait_ge(s[f"gp{d}"], c0[f"gp{d}"] + gv(PE_SIG, g, f"w{k}"))
                        sig(d, dve.tensor_tensor(gW[d][:, :, :], heads(bank[4 * d]), per_mat(con(f"level{k}")), ALU.mult))
                    for d, t in pair:
                        last = k == LV - 1
                        dve.wait_ge(s[f"gp{d}"], c0[f"gp{d}"] + gv(PE_SIG, g, "f6" if last else f"t{k}"))
                        dst, b = (gY[d], 1) if last and d else (gYT[d], 2)
                        sig(d, dve.tensor_copy(dst[:, :, :], heads(bank[4 * d + b])))
                for d, t in pair:
                    v = vrow[:, t, :].rearrange("p (h j) -> p h j", j=P)
                    dve.wait_ge(s[f"gp{d}"], c0[f"gp{d}"] + gv(PE_SIG, g, "ks"))
                    link(dve.tensor_tensor(gE[d][:, :, :], v, per_row(beta, t, 4 * d, HA), ALU.mult))
                    link(dve.tensor_tensor(gN[d][:, :, :], heads(bank[4 * d]), per_row(nbg, t, 4 * d, HA), ALU.mult))
                    sig(d, dve.tensor_tensor(gN[d][:, :, :], gN[d][:, :, :], gE[d][:, :, :], ALU.add))
                for d, t in pair:
                    dve.wait_ge(s[f"ga{d}"], c0[f"ga{d}"] + gv(AC_SIG, g, "vn"))
                    mine(d, "r")
                    sig(d, dve.tensor_tensor(gE[d][:, :, :], gNT[d][:, :, :], per_row(ek, t, 4 * d, HA), ALU.mult))
                for d, t in pair:
                    o = orow[:, t, :].rearrange("p (h j) -> p h j", j=P)
                    dve.wait_ge(s[f"gp{d}"], c0[f"gp{d}"] + gv(PE_SIG, g, "qs"))
                    link(dve.tensor_tensor(gN[d][:, :, :], heads(bank[4 * d + 1]), per_row(eg, t, 4 * d, HA), ALU.mult))
                    link(dve.tensor_tensor(gN[d][:, :, :], heads(bank[4 * d + 2]), gN[d][:, :, :], ALU.add))
                    sig(d, dve.tensor_tensor(o, o, gN[d][:, :, :], ALU.add))
                for d, t in pair:
                    st = state[:, 4 * d:4 * d + 4, :]
                    dve.wait_ge(s[f"gp{d}"], c0[f"gp{d}"] + gv(PE_SIG, g, "kv"))
                    link(dve.tensor_tensor(st, st, per_row(egt, t, 4 * d, HA), ALU.mult))
                    sig(d, dve.tensor_tensor(st, heads(bank[4 * d]), st, ALU.add))
                for d, t in pair:
                    mine(d, "state")

            def row_copy(s, c0, kind, h):
                n = TURNS.index((kind, h))
                dve.wait_ge(s["tr_mm"], c0["tr_mm"] + n + 1)
                dst = vrow if kind == "v" else krow
                dve.tensor_copy(dst[:, :, h * P:(h + 1) * P], bank[6 + n % 2][:, :].rearrange("p (t j) -> p t j", j=P)).then_inc(s["tr_ev"], 1)

            def rope():
                hh = HB + GB
                for t in (2, 3):
                    x = arow[:, t, A_Q:A_V]
                    x5 = x.rearrange("p (h a b c) -> p (h a) b c", a=2, b=2, c=16)
                    t5 = rtmp[:, t - 2, :].rearrange("p (h a b c) -> p (h a) b c", a=2, b=2, c=16)
                    sn = con(f"sin{t - 2}").rearrange("p (a b c) -> p a b c", a=2, b=2)
                    for h in range(hh):
                        for b in range(2):
                            last = dve.tensor_tensor(t5[:, 2 * h:2 * h + 2, b, :], x5[:, 2 * h:2 * h + 2, 1 - b, :], sn[:, :, b, :], ALU.mult)
                    link(last)
                    cs = con(f"cos{t - 2}").rearrange("p (o n) -> p o n", o=1).to_broadcast([P, hh, DH])
                    xh = x.rearrange("p (h n) -> p h n", n=DH)
                    link(dve.tensor_tensor(xh, xh, cs, ALU.mult))
                    link(dve.tensor_tensor(x, x, rtmp[:, t - 2, :], ALU.add))
                link(dve.tensor_copy(kswap[:, :, 0:DH], arow[:, :, A_K + DH:A_K + 2 * DH]))
                link(dve.tensor_copy(kswap[:, :, DH:2 * DH], arow[:, :, A_K:A_K + DH]))

            def o_squares(l, s, c0):
                t0, nn = active(l)[0], 4 * len(active(l))
                o = orow[:, t0:, :].rearrange("p t (h j) -> p (t h) j", j=P)
                link(dve.tensor_tensor(gsq[:, 0:nn, :], o, o, ALU.mult))
                dve.tensor_reduce(ss[:, 0:nn], gsq[:, 0:nn, :], AX.X, ALU.add).then_inc(s["o_sq"], 1)

            def o_scale(l, s, c0, j):
                t = active(l)[j]
                o = orow[:, t, :].rearrange("p (h j) -> p h j", j=P)
                z = zrow[:, t, :].rearrange("p (h j) -> p h j", j=P)
                link(dve.tensor_tensor(o, o, rstd[:, 4 * j:4 * j + 4].rearrange("p (h o) -> p h o", o=1).to_broadcast([P, HA, P]), ALU.mult))
                link(dve.tensor_tensor(o, o, per_mat(gdn_g[:, l, :]), ALU.mult))
                dve.tensor_tensor(o, o, z, ALU.mult).then_inc(s["o_ya"], 1)

            def attention(l, s, c0):
                dve.wait_ge(s["kt_mm"], c0["kt_mm"] + 1)
                link(dve.tensor_copy(kTA, bank[0][:, :]))
                dve.tensor_copy(kTB, bank[1][:, :]).then_inc(s["kt_ev"], 1)
                for j, t in enumerate(active(l)):
                    dve.wait_ge(s["kt_mm"], c0["kt_mm"] + 2 + j)
                    dve.tensor_copy(qT[:, t, :], bank[2 + j][:, :]).then_inc(s["kt_ev"], 1)
                units = att_units(l)
                for n in range(len(units) + 2):
                    if n < len(units):
                        j, t, h, keys, masked = units[n]
                        sc = bank[n % 2]
                        dve.wait_ge(s["at_s"], c0["at_s"] + n + 1)
                        if masked is not None:
                            m = sc[:, masked * P:(masked + 1) * P]
                            link(dve.tensor_tensor(m, m, con(f"band{t - 2}"), ALU.add))
                        link(dve.reduce_max(mx[:, t, h:h + 1], sc[:, 0:keys], AX.X))
                        dve.tensor_scalar(nm[:, t, h:h + 1], mx[:, t, h:h + 1], -SCALE, nsink[:, l, h:h + 1],
                                          ALU.mult, ALU.min).then_inc(s["at_nm"], 1)
                    if n == 1:
                        o_squares(l, s, c0)
                    if n == 3:
                        dve.wait_ge(s["o_rs"], c0["o_rs"] + 1)
                        newton(4 * len(active(l)), 1.0 / P)
                    if n >= 4 and n % 2 == 0 and n // 2 - 2 < len(active(l)):
                        o_scale(l, s, c0, n // 2 - 2)
                    if 1 <= n <= len(units):
                        m = n - 1
                        keys = units[m][3]
                        dve.wait_ge(s["at_tr"], c0["at_tr"] + m + 1)
                        if m >= 2:
                            dve.wait_ge(s["at_o"], c0["at_o"] + m - 1)
                        dve.tensor_copy(probT[:, m % 2, 0:keys], bank[2 + m % 2][:, 0:keys]).then_inc(s["at_tev"], 1)
                    if n >= 2 and units[n - 2][2] == HB - 1:
                        m = n - 2
                        j, t = units[m][:2]
                        dve.wait_ge(s["at_o"], c0["at_o"] + m + 1)
                        link(dve.tensor_tensor(den[:, t, :], den[:, t, :], esk[:, t, :], ALU.add))
                        link(dve.reciprocal(den[:, t, :], den[:, t, :]))
                        dve.tensor_tensor(yb[:, t, :].rearrange("p (h d) -> p h d", d=DH),
                                          bank[4 + j % 2][:, :].rearrange("p (h d) -> p h d", d=DH),
                                          den[:, t, :].rearrange("p (h o) -> p h o", o=1).to_broadcast([P, HB, DH]),
                                          ALU.mult).then_inc(s["at_y"], 1)

            def merge(l, s, c0):
                act_t = active(l)
                n = 0
                for dst in (yaT, ybT):
                    for t in act_t:
                        dve.wait_ge(s["mT_mm"], c0["mT_mm"] + n + 1)
                        dve.tensor_copy(dst[:, :, t * P:(t + 1) * P], bank[6 + n % 2][:, :].rearrange("p (k j) -> p k j", j=P)).then_inc(s["mT_ev"], 1)
                        n += 1
                nact = len(act_t)
                for half in range(2):
                    for step, x in enumerate((ga, gb)):
                        for j in range(nact):
                            dve.wait_ge(s["mg_a"], c0["mg_a"] + (2 * half + step) * nact + j + 1)
                            link(dve.tensor_scalar(x[:, j, :], x[:, j, :], 1.0, None, ALU.add))
                            link(dve.reciprocal(x[:, j, :], x[:, j, :]))
                    for step, x in enumerate((ga, gb)):
                        for j, t in enumerate(act_t):
                            n = (4 * half + 2 + step) * nact + j
                            m = mrow[:, t, half * 512:(half + 1) * 512]
                            dve.wait_ge(s["mg_mm"], c0["mg_mm"] + n + 1)
                            if step == 0:
                                dve.tensor_tensor(m, bank[n % 8][:, :], x[:, j, :], ALU.mult).then_inc(s["mg_d"], 1)
                            else:
                                link(dve.tensor_tensor(pa[:, j % 2, :], bank[n % 8][:, :], x[:, j, :], ALU.mult))
                                dve.tensor_tensor(m, m, pa[:, j % 2, :], ALU.add).then_inc(s["mg_d"], 1)
                for j, t in enumerate(act_t):
                    for q in range(2):
                        dve.wait_ge(s["m2_mm"], c0["m2_mm"] + 2 * j + q + 1)
                        dve.tensor_copy(HT[:, 4 * q:4 * q + 4, t * P:(t + 1) * P],
                                        bank[2 * (j % 2) + q][:, :].rearrange("p (k j) -> p k j", j=P)).then_inc(s["m2_ev"], 1)
                dve.wait_ge(s["g1load"], c0["g1load"] + 32)
                n = 0
                for half in range(2):
                    cs = slice(half * 512, (half + 1) * 512)
                    for t in act_t:
                        dve.wait_ge(s["y_mm"], c0["y_mm"] + n + 1)
                        link(dve.tensor_tensor(pa[:, n % 2, :], bank[4 + n % 2][:, :], g1bc[:, stream(t), cs], ALU.mult))
                        dve.tensor_tensor(X[:, t, cs], X[:, t, cs], pa[:, n % 2, :], ALU.add).then_inc(s["y_ev"], 1)
                        n += 1

            def norm2(l, s, c0):
                act_t = active(l)
                nn = len(act_t)
                dve.wait_ge(s["n2rs0"], c0["n2rs0"] + 1)
                newton(nn, 1.0 / D)
                dve.wait_ge(s["bcload"], c0["bcload"] + 80)
                for j in range(nn + 1):
                    if j < nn:
                        t = act_t[j]
                        link(dve.scalar_tensor_tensor(out=h2[:, j, :], in0=X[:, t, :], scalar=rstd[:, j:j + 1], in1=g2n[:, stream(t), :],
                                                      op0=ALU.mult, op1=ALU.mult))
                        dve.tensor_tensor(h2[:, j, :], h2[:, j, :], sh2bc[:, stream(t), :], ALU.add).then_inc(s["h2row"], 1)
                    if j >= 1:
                        q = j - 1
                        dve.wait_ge(s["r_tr"], c0["r_tr"] + q + 1)
                        if q >= 2:
                            dve.wait_ge(s["r_mm"], c0["r_mm"] + q - 1)
                        dve.tensor_copy(h2T[:, q % 2, 0:512], bank[4 * (q % 2)][:, :])
                        dve.tensor_copy(h2T[:, q % 2, 512:1024], bank[4 * (q % 2) + 1][:, :]).then_inc(s["r_tev"], 1)

            def route(l, s, c0):
                act_t = active(l)
                nn = len(act_t)
                t0 = act_t[0]
                A = lambda x: x[:, 0:nn, :]
                B1 = lambda x, n: x[:, 0:nn].rearrange("p (t o) -> p t o", o=1).to_broadcast([P, nn, n])
                row = lambda x, n: x.rearrange("p (o e) -> p o e", o=1).to_broadcast([P, nn, n])
                score, sel, msel, oh1, oh2, hot, key, rank = (rt[i] for i in (1, 2, 3, 4, 6, 5, 7, 8))
                dve.wait_ge(s["r_a"], c0["r_a"] + 1)
                link(dve.tensor_scalar(A(score), A(rt[0]), 1.0, None, ALU.add))
                link(dve.reciprocal(A(score), A(score)))
                link(dve.tensor_tensor(A(sel), A(score), row(rbias, NE), ALU.add))
                s4 = A(sel).rearrange("p t (g e) -> p (t g) e", e=4)
                pr = rp[:, 0:nn, :, :].rearrange("p t g e -> p (t g) e")
                dve.tensor_tensor(pr[:, :, 0:3], s4[:, :, 0:3], s4[:, :, 1:4], ALU.add)
                dve.tensor_tensor(pr[:, :, 3:5], s4[:, :, 0:2], s4[:, :, 2:4], ALU.add)
                link(dve.tensor_tensor(pr[:, :, 5:6], s4[:, :, 0:1], s4[:, :, 3:4], ALU.add))
                link(dve.reduce_max(A(rg[0]).rearrange("p t g -> p (t g)"), pr, AX.X))
                link(dve.reduce_max(r1[0][:, 0:nn], A(rg[0]), AX.X))
                link(dve.tensor_tensor(A(rg[1]), A(rg[0]), B1(r1[0], NG), ALU.is_equal))
                link(dve.tensor_tensor(A(rg[1]), A(rg[1]), row(con("grouprank"), NG), ALU.mult))
                link(dve.reduce_max(r1[0][:, 0:nn], A(rg[1]), AX.X))
                link(dve.tensor_tensor(A(rg[1]), A(rg[1]), B1(r1[0], NG), ALU.is_equal))
                link(dve.tensor_copy(A(key).rearrange("p t (g e) -> p (t g) e", e=4),
                                     A(rg[1]).rearrange("p t (g o) -> p (t g) o", o=1).to_broadcast([P, nn * NG, 4])))
                link(dve.tensor_tensor(A(msel), A(sel), A(key), ALU.mult))
                link(dve.tensor_scalar(A(key), A(key), 1e30, -1e30, ALU.mult, ALU.add))
                link(dve.tensor_tensor(A(msel), A(msel), A(key), ALU.add))
                for oh in (oh1, oh2):
                    link(dve.reduce_max(r1[0][:, 0:nn], A(msel), AX.X))
                    link(dve.tensor_tensor(A(key), A(msel), B1(r1[0], NE), ALU.is_equal))
                    link(dve.tensor_tensor(A(key), A(key), row(con("expertrank"), NE), ALU.mult))
                    link(dve.reduce_max(r1[0][:, 0:nn], A(key), AX.X))
                    link(dve.tensor_tensor(A(oh), A(key), B1(r1[0], NE), ALU.is_equal))
                    link(dve.scalar_tensor_tensor(out=A(msel), in0=A(oh), scalar=-1e31, in1=A(msel), op0=ALU.mult, op1=ALU.add))
                dve.tensor_tensor(A(hot), A(oh1), A(oh2), ALU.add).then_inc(s["r_hot"], 1)
                for j, oh in enumerate((oh1, oh2)):
                    link(dve.tensor_tensor(A(key), A(oh), A(score), ALU.mult))
                    link(dve.reduce_sum(r1[1 + j][:, 0:nn], A(key), AX.X))
                link(dve.tensor_tensor(r1[3][:, 0:nn], r1[1][:, 0:nn], r1[2][:, 0:nn], ALU.add))
                link(dve.reciprocal(r1[3][:, 0:nn], r1[3][:, 0:nn]))
                for j in range(2):
                    link(dve.tensor_tensor(wkeep[:, j, 0:nn], r1[1 + j][:, 0:nn], r1[3][:, 0:nn], ALU.mult))
                dve.wait_ge(s["r_rank"], c0["r_rank"] + 1)
                cnt, nb, inc, start, tmp, one = re
                link(dve.tensor_copy(cnt, bank[4][:, 0:NE]))
                link(dve.tensor_scalar(nb, cnt, 0.0, None, ALU.is_gt))
                for k in range(1, nn):
                    link(dve.tensor_scalar(tmp, cnt, float(P * k), None, ALU.is_gt))
                    link(dve.tensor_tensor(nb, nb, tmp, ALU.add))
                link(dve.memset(one, 1.0))
                link(dve.tensor_tensor_scan(inc, one, nb, 0.0, ALU.mult, ALU.add))
                link(dve.tensor_tensor(start, inc, nb, ALU.subtract))
                link(dve.tensor_tensor(cmpb[:, :, :], con("iota")[:, 0:NBLK].rearrange("p (b o) -> p b o", o=1).to_broadcast([P, NBLK, NE]),
                                       start.rearrange("p (o e) -> p o e", o=1).to_broadcast([P, NBLK, NE]), ALU.is_ge))
                link(dve.reduce_sum(blk_e[:, 0:NBLK], cmpb[:, :, :], AX.X))
                link(dve.tensor_scalar(blk_e[:, 0:NBLK], blk_e[:, 0:NBLK], -1.0, None, ALU.add))
                link(dve.tensor_copy(blk_e[:, NBLK:NBLK + 1], inc[:, NE - 1:NE]))
                dve.tensor_copy(meta[:, :], blk_e).then_inc(s["blocks"], 1)
                link(dve.tensor_scalar(tmp, start, float(P), None, ALU.mult))
                link(dve.tensor_tensor(A(rank), bank[3][:, 0:nn * NE].rearrange("p (t e) -> p t e", e=NE), row(tmp, NE), ALU.add))
                for j, oh in enumerate((oh1, oh2)):
                    link(dve.tensor_tensor(A(key), A(oh), A(rank), ALU.mult))
                    link(dve.reduce_sum(r1[4 + j][:, 0:nn], A(key), AX.X))
                    link(dve.tensor_copy(pos_u[:, j, t0:NT], r1[4 + j][:, 0:nn]))
                    link(dve.tensor_copy(pos_i[:, 0, j, 0:nn], r1[4 + j][:, 0:nn]))
                    link(dve.tensor_scalar(pos_i[:, 1, j, 0:nn], pos_i[:, 0, j, 0:nn], P - 1, None, ALU.bitwise_and))
                    link(dve.tensor_scalar(pos_i[:, 2, j, 0:nn], pos_i[:, 0, j, 0:nn], 7, None, ALU.logical_shift_right))
                    link(dve.tensor_copy(r1[6 + j][:, 0:nn], pos_i[:, 1, j, 0:nn]))
                    link(dve.tensor_copy(r1[8 + j][:, 0:nn], pos_i[:, 2, j, 0:nn]))
                for j in range(2):
                    for t in range(nn):
                        q = 2 * t + j
                        dve.tensor_scalar(hot_r[:, q, :], con("iota"), r1[6 + j][:, t:t + 1], None, ALU.is_equal)
                        last = dve.tensor_scalar(hot_b[:, q, :], con("iota")[:, 0:NBLK], r1[8 + j][:, t:t + 1],
                                                 con("token")[:, t0 + t:t0 + t + 1], ALU.is_equal, ALU.mult)
                last.then_inc(s["r_sort"], 1)
                dve.wait_ge(s["r_inv"], c0["r_inv"] + 1)
                dve.tensor_copy(slot_tok[:, 0:NBLK], bank[5][:, 0:NBLK]).then_inc(s["routed"], 1)

            def experts(l, s, c0):
                nblk = dve.value_load(meta[0:1, NBLK:NBLK + 1], min_val=1, max_val=NBLK)
                dve.sem_inc(s["ed_ev0"], 1)
                dve.wait_ge(s["xg_mm0"], 1)
                dve.tensor_copy(xT[:, 0, 0:512], bank[0][:, :]).then_inc(s["xg_ev0"], 1)
                with dve.Fori(0, NBLK // 2) as i:
                    for u in range(2):
                        b = i * 2 + u
                        with dve.If(b < nblk):
                            dve.wait_ge(s["eu_mm"], b + 3)
                            dve.wait_ge(s["e_silu"], b + 1)
                            dve.tensor_tensor(he[:, u, :], bank[3][:, :], eg_s[:, u, :], ALU.mult).then_inc(s["e_he"], 1)
                            dve.wait_ge(s["xg_mm0"], b + 2)
                            dve.tensor_copy(xT[:, 1 - u, 0:512], bank[0][:, :]).then_inc(s["xg_ev0"], 1)
                            dve.wait_ge(s[f"st{u}"], (i + 1) * 16)
                            dve.wait_ge(s["ed_mm"], b + 3)
                            dve.tensor_copy(yrow[:, u, 0:512], bank[5][:, :]).then_inc(s["ed_ev0"], 1)

            def combine(l, s, c0):
                act_t = active(l)
                if l == 0:
                    dve.wait_ge(S[1]["b_load"], before[1]["b_load"] + 96)
                    dve.wait_ge(S[1]["modev"], before[1]["modev"] + MOD_EARLY)
                    fold(1, 1)
                dve.wait_ge(s["g2load"], c0["g2load"] + 32)
                for j, t in enumerate(act_t):
                    dve.wait_ge(s[f"ygl{j}"], c0[f"ygl{j}"] + 32)
                    y1, y2 = yg[:, 2 * j, :], yg[:, 2 * j + 1, :]
                    link(dve.tensor_scalar(y1, y1, wkeep[:, 0, j:j + 1], None, ALU.mult))
                    link(dve.scalar_tensor_tensor(out=y1, in0=y2, scalar=wkeep[:, 1, j:j + 1], in1=y1, op0=ALU.mult, op1=ALU.add))
                    link(dve.tensor_tensor(y1, y1, g2bc[:, stream(t), :], ALU.mult))
                    dve.tensor_tensor(X[:, t, :], X[:, t, :], y1, ALU.add).then_inc(s["comb"], 1)
                if l == DEPTH - 1:
                    dve.wait_ge(once["f_rs"], 1)
                    newton(2, 1.0 / D)
                    dve.wait_ge(fin_load, 16)
                    for j, t in enumerate(act_t):
                        dve.scalar_tensor_tensor(out=X[:, t, :], in0=X[:, t, :], scalar=rstd[:, j:j + 1], in1=fg,
                                                 op0=ALU.mult, op1=ALU.mult).then_inc(once["f_out"], 1)

            for l in range(DEPTH):
                layer(l)


_INS = ["x", "c", "ctx", "c_ctx", "w_mod", "b_mod", "norm1_g", "norm2_g", "w_in", "conv_w", "a_log", "dt_bias",
        "gdn_norm_g", "sink", "w_oa", "w_ob", "w_o", "w_router", "router_bias", "w_gate", "w_up", "w_down", "final_g"]


def kernel(**inputs):
    import concourse.bacc as _bacc
    from concourse.bass_utils import run_bass_kernel_spmd as _run

    nc = _bacc.Bacc("TRN2", target_bir_lowering=False, num_devices=1)
    arrays, args = {}, {}
    for name in _INS:
        v = np.ascontiguousarray(inputs[name])
        arrays[f"in_{name}"] = v
        args[name] = nc.dram_tensor(f"in_{name}", v.shape, mybir.dt.from_np(v.dtype), kind="ExternalInput").ap()
    table = np.ascontiguousarray(constants()[0])
    arrays["in_table"] = table
    args["table"] = nc.dram_tensor("in_table", table.shape, F32, kind="ExternalInput").ap()
    out = nc.dram_tensor("out_0", (1, SEQ, D), F32, kind="ExternalOutput").ap()
    build(nc, args, out)
    r = _run(nc, [arrays], core_ids=[0])
    return r.results[0]["out_0"]
```
